# Optimizing a Trainium2 kernel written in Bass

```python
import math
import jax, jax.numpy as jnp
from jax import lax
import numpy as np

D_MODEL = 1024
BATCH = 1
SEQ = 512
DEPTH = 2

MIX_WIDTH = D_MODEL
GM_HEADS = 4
GM_HEAD_DIM = D_MODEL // 16
GM_WIDTH = GM_HEADS * GM_HEAD_DIM
GM_CHUNK = 128
MLA_HEADS = 8
MLA_NOPE = D_MODEL // 16
MLA_ROPE = D_MODEL // 32
MLA_V = D_MODEL // 16
MLA_WIDTH = MLA_HEADS * MLA_V
MLA_Q_RANK = D_MODEL // 4
MLA_KV_RANK = D_MODEL // 8
ROPE_THETA = 10000.0
ATTN_BLOCK = 128
MASK_VALUE = -1e30
HG_HEADS = 4
HG_KEY = D_MODEL // 16
HG_VAL = D_MODEL // 16
HG_KEY_WIDTH = HG_HEADS * HG_KEY
HG_WIDTH = HG_HEADS * HG_VAL
HG_CHUNK = 64
GATE_FLOOR = 1e-20
IN_WIDTHS = (GM_WIDTH, GM_WIDTH, MLA_Q_RANK, MLA_KV_RANK, MLA_ROPE,
             HG_KEY_WIDTH, HG_KEY_WIDTH, HG_WIDTH, HG_WIDTH)
IN_WIDTH = 2 * GM_WIDTH + MLA_Q_RANK + MLA_KV_RANK + MLA_ROPE + 2 * HG_KEY_WIDTH + 2 * HG_WIDTH
PEER_HEADS = 8
PEER_N_KEYS = 128
PEER_N_EXPERTS = PEER_N_KEYS * PEER_N_KEYS
PEER_TOPK = 16
PEER_QDIM = D_MODEL // 8
PEER_BLOCK = 128
NORM_EPS = 1e-6

kernel_name = "hymba_gmlp_mla_hgrn2_peer_trunk"

F32 = jnp.float32

def rmsnorm(x, g):
    xf = x.astype(F32)
    y = xf * lax.rsqrt(jnp.mean(xf * xf, axis=-1, keepdims=True) + NORM_EPS)
    return (y * g.astype(F32)).astype(x.dtype)

def head_rmsnorm(x, g, n_heads):
    shp = x.shape
    d = shp[-1] // n_heads
    y = rmsnorm(x.reshape(shp[:-1] + (n_heads, d)), g.reshape(n_heads, d))
    return y.reshape(shp)

def apply_rope(x, positions):
    half = MLA_ROPE // 2
    inv_freq = jnp.exp(-math.log(ROPE_THETA) * jnp.arange(half, dtype=F32) / half)
    ang = positions.astype(F32)[..., None] * inv_freq
    ang = ang.reshape(ang.shape[:2] + (1,) * (x.ndim - 3) + (half,))
    cos, sin = jnp.cos(ang), jnp.sin(ang)
    xf = x.astype(F32)
    x1, x2 = xf[..., :half], xf[..., half:]
    return jnp.concatenate([x1 * cos - x2 * sin, x2 * cos + x1 * sin], axis=-1).astype(x.dtype)

def chunked_gmlp(u, v, v_gain, w_s, b_s):
    B, S, _ = u.shape
    u = jax.nn.gelu(u)
    v = head_rmsnorm(jax.nn.gelu(v), v_gain, GM_HEADS)
    v = v.reshape(B, S // GM_CHUNK, GM_CHUNK, GM_HEADS, GM_HEAD_DIM)
    causal = jnp.tril(jnp.ones((GM_CHUNK, GM_CHUNK), dtype=bool))
    w = jnp.where(causal, w_s, 0).astype(v.dtype)
    z = jnp.einsum('hts,bcshd->bcthd', w, v) + b_s.T.astype(v.dtype)[None, None, :, :, None]
    return u * z.reshape(B, S, GM_WIDTH)

def mla(c_q, c_kv, k_rope, positions, q_norm, w_uq, kv_norm, w_ukv):
    B, S, _ = c_q.shape
    q = (rmsnorm(c_q, q_norm) @ w_uq).reshape(B, S, MLA_HEADS, MLA_NOPE + MLA_ROPE)
    q_nope = q[..., :MLA_NOPE]
    q_rope = apply_rope(q[..., MLA_NOPE:], positions)
    kv = (rmsnorm(c_kv, kv_norm) @ w_ukv).reshape(B, S, MLA_HEADS, MLA_NOPE + MLA_V)
    k_nope, v = kv[..., :MLA_NOPE], kv[..., MLA_NOPE:]
    k_rope = apply_rope(k_rope, positions)
    scale = (MLA_NOPE + MLA_ROPE) ** -0.5
    nb = S // ATTN_BLOCK
    qn_b = q_nope.reshape(B, nb, ATTN_BLOCK, MLA_HEADS, MLA_NOPE).transpose(1, 0, 2, 3, 4)
    qr_b = q_rope.reshape(B, nb, ATTN_BLOCK, MLA_HEADS, MLA_ROPE).transpose(1, 0, 2, 3, 4)
    k_pos = jnp.arange(S)

    def block(args):
        qn, qr, i = args
        s = jnp.einsum('bqhd,bkhd->bhqk', qn, k_nope) + jnp.einsum('bqhr,bkr->bhqk', qr, k_rope)
        s = s.astype(F32) * scale
        q_pos = i * ATTN_BLOCK + jnp.arange(ATTN_BLOCK)
        s = jnp.where(k_pos[None, :] <= q_pos[:, None], s, MASK_VALUE)
        p = jax.nn.softmax(s, axis=-1).astype(v.dtype)
        return jnp.einsum('bhqk,bkhd->bqhd', p, v)

    o = lax.map(block, (qn_b, qr_b, jnp.arange(nb)))
    return o.transpose(1, 0, 2, 3, 4).reshape(B, S, MLA_WIDTH)

def hgrn_lower_bounds(logits):
    p = jax.nn.softmax(logits.astype(F32), axis=0)
    return jnp.cumsum(p, axis=0) - p[0]

def hgrn2(q, f, i, g, lb, out_norm):
    B, S, _ = q.shape
    dt = i.dtype
    C, nc = HG_CHUNK, S // HG_CHUNK
    qf = jax.nn.silu(q.astype(F32)).reshape(B, S, HG_HEADS, HG_KEY)
    fx = f.astype(F32).reshape(B, S, HG_HEADS, HG_KEY)
    lbh = lb.reshape(HG_HEADS, HG_KEY)
    f_gate = lbh + (1.0 - lbh) * jax.nn.sigmoid(fx)
    log_f = jnp.log(jnp.maximum(f_gate, GATE_FLOOR))
    kf = (1.0 - lbh) * jax.nn.sigmoid(-fx)
    vf = i.astype(F32).reshape(B, S, HG_HEADS, HG_VAL)

    def to_chunks(t):
        return t.reshape(B, nc, C, HG_HEADS, t.shape[-1]).transpose(1, 0, 3, 2, 4)

    causal = jnp.tril(jnp.ones((C, C), dtype=bool))[:, :, None]

    def step(state, inp):
        qc, kc, vc, lfc = inp
        b = jnp.cumsum(lfc, axis=2)
        o_inter = jnp.einsum('bhtk,bhkv->bhtv', qc * jnp.exp(b), state)
        diff = b[:, :, :, None, :] - b[:, :, None, :, :]
        decay = jnp.where(causal, jnp.exp(jnp.where(causal, diff, 0.0)), 0.0)
        a = jnp.einsum('bhtk,bhsk,bhtsk->bhts', qc, kc, decay)
        o_intra = jnp.einsum('bhts,bhsv->bhtv', a, vc)
        b_last = b[:, :, -1:, :]
        new_state = jnp.exp(b_last[:, :, 0, :])[..., None] * state + \
            jnp.einsum('bhsk,bhsv->bhkv', kc * jnp.exp(b_last - b), vc)
        return new_state, o_inter + o_intra

    s0 = jnp.zeros((B, HG_HEADS, HG_KEY, HG_VAL), F32)
    _, o = lax.scan(step, s0, (to_chunks(qf), to_chunks(kf), to_chunks(vf), to_chunks(log_f)))
    o = o.transpose(1, 0, 3, 2, 4).reshape(B, S, HG_WIDTH)
    o = head_rmsnorm(o, out_norm, HG_HEADS) * jax.nn.silu(g.astype(F32))
    return o.astype(dt)

def peer(xn, w_q, sub_keys, u_tab, v_tab):
    B, S, D = xn.shape
    xb = xn.reshape((B * S) // PEER_BLOCK, PEER_BLOCK, D)
    K = PEER_TOPK

    def block(xt):
        q = (xt @ w_q).reshape(PEER_BLOCK, PEER_HEADS, 2, PEER_QDIM // 2)
        s = jnp.einsum('thpd,hpkd->thpk', q, sub_keys).astype(F32)
        s_top, i_top = lax.top_k(s, K)
        cand_s = (s_top[:, :, 0, :, None] + s_top[:, :, 1, None, :]).reshape(PEER_BLOCK, PEER_HEADS, K * K)
        cand_i = (i_top[:, :, 0, :, None] * PEER_N_KEYS + i_top[:, :, 1, None, :]).reshape(PEER_BLOCK, PEER_HEADS, K * K)
        best_s, pos = lax.top_k(cand_s, K)
        ids = jnp.take_along_axis(cand_i, pos, axis=-1)
        gate = jax.nn.softmax(best_s, axis=-1).astype(xt.dtype)
        u = jnp.take(u_tab, ids, axis=0)
        act = jax.nn.gelu(jnp.einsum('td,thkd->thk', xt, u))
        vv = jnp.take(v_tab, ids, axis=0)
        return jnp.einsum('thk,thkd->td', gate * act, vv)

    return lax.map(block, xb).reshape(B, S, D)

def setup_inputs(seed: int = 0) -> dict:
    key = jax.random.key(seed)
    ks = jax.random.split(key, 24)
    nrm = lambda k, shape, s: jax.random.normal(k, shape, F32) * s
    gain = lambda k, shape: 1.0 + 0.02 * jax.random.normal(k, shape, F32)
    x = jax.random.normal(ks[0], (BATCH, SEQ, D_MODEL), F32)
    offset = jax.random.randint(ks[1], (BATCH, 1), 0, SEQ, dtype=jnp.int32)
    positions = (jnp.arange(SEQ, dtype=jnp.int32)[None, :] + offset).astype(jnp.int32)
    return {
        "x": x,
        "positions": positions,
        "norm_mix": gain(ks[2], (DEPTH, D_MODEL)),
        "w_in": nrm(ks[3], (DEPTH, D_MODEL, IN_WIDTH), D_MODEL ** -0.5),
        "gm_v_norm": gain(ks[4], (DEPTH, GM_WIDTH)),
        "gm_ws": nrm(ks[5], (DEPTH, GM_HEADS, GM_CHUNK, GM_CHUNK), 0.5 * GM_CHUNK ** -0.5),
        "gm_b": 1.0 + 0.1 * jax.random.normal(ks[6], (DEPTH, GM_HEADS, GM_CHUNK), F32),
        "gm_out_norm": gain(ks[7], (DEPTH, GM_WIDTH)),
        "mla_q_norm": gain(ks[8], (DEPTH, MLA_Q_RANK)),
        "mla_w_uq": nrm(ks[9], (DEPTH, MLA_Q_RANK, MLA_HEADS * (MLA_NOPE + MLA_ROPE)), MLA_Q_RANK ** -0.5),
        "mla_kv_norm": gain(ks[10], (DEPTH, MLA_KV_RANK)),
        "mla_w_ukv": nrm(ks[11], (DEPTH, MLA_KV_RANK, MLA_HEADS * (MLA_NOPE + MLA_V)), MLA_KV_RANK ** -0.5),
        "mla_out_norm": gain(ks[12], (DEPTH, MLA_WIDTH)),
        "hg_lb_logits": nrm(ks[13], (DEPTH, HG_KEY_WIDTH), 0.5),
        "hg_out_norm": gain(ks[14], (DEPTH, HG_WIDTH)),
        "w_out": nrm(ks[15], (DEPTH, MIX_WIDTH, D_MODEL), MIX_WIDTH ** -0.5),
        "norm_ffn": gain(ks[16], (DEPTH, D_MODEL)),
        "peer_w_q": nrm(ks[17], (DEPTH, D_MODEL, PEER_HEADS * PEER_QDIM), D_MODEL ** -0.5),
        "peer_sub_keys": nrm(ks[18], (DEPTH, PEER_HEADS, 2, PEER_N_KEYS, PEER_QDIM // 2), (PEER_QDIM // 2) ** -0.5),
        "peer_u": nrm(ks[19], (DEPTH, PEER_N_EXPERTS, D_MODEL), D_MODEL ** -0.5),
        "peer_v": nrm(ks[20], (DEPTH, PEER_N_EXPERTS, D_MODEL), PEER_HEADS ** -0.5),
        "norm_final": gain(ks[21], (D_MODEL,)),
    }

def reference(x, positions, norm_mix, w_in, gm_v_norm, gm_ws, gm_b, gm_out_norm,
              mla_q_norm, mla_w_uq, mla_kv_norm, mla_w_ukv, mla_out_norm,
              hg_lb_logits, hg_out_norm, w_out, norm_ffn, peer_w_q, peer_sub_keys,
              peer_u, peer_v, norm_final):
    split_points = [int(s) for s in np.cumsum(IN_WIDTHS)[:-1]]
    lower_bounds = hgrn_lower_bounds(hg_lb_logits)
    for l in range(DEPTH):
        n = rmsnorm(x, norm_mix[l])
        proj = n @ w_in[l]
        u, v, c_q, c_kv, k_rope, hq, hf, hi, hg = jnp.split(proj, split_points, axis=-1)
        y_a = head_rmsnorm(chunked_gmlp(u, v, gm_v_norm[l], gm_ws[l], gm_b[l]), gm_out_norm[l], GM_HEADS)
        y_b = head_rmsnorm(mla(c_q, c_kv, k_rope, positions, mla_q_norm[l], mla_w_uq[l],
                               mla_kv_norm[l], mla_w_ukv[l]), mla_out_norm[l], MLA_HEADS)
        y_c = hgrn2(hq, hf, hi, hg, lower_bounds[l], hg_out_norm[l])
        x = x + jnp.concatenate([y_a, y_b, y_c], axis=-1) @ w_out[l]
        x = x + peer(rmsnorm(x, norm_ffn[l]), peer_w_q[l], peer_sub_keys[l], peer_u[l], peer_v[l])
    return rmsnorm(x, norm_final)


_drawn_inputs = setup_inputs


def setup_inputs(seed=0):
    import zlib

    import numpy as np

    out = dict(_drawn_inputs(seed))
    spreads = {}
    factors = {'gm_v_norm': 20.392,
     'hg_lb_logits': 2.81,
     'hg_out_norm': 3.713,
     'norm_final': 7.462,
     'gm_out_norm': 3.545,
     'mla_q_norm': 3.101,
     'mla_out_norm': 2.763}
    for name, (base, spread) in spreads.items():
        noise = np.random.default_rng([zlib.crc32(name.encode()), seed]).standard_normal(out[name].shape)
        drawn = base * np.exp(spread * noise) if base else spread * noise
        out[name] = __import__('jax').numpy.asarray(drawn.astype(out[name].dtype))
    for name, factor in factors.items():
        out[name] = (out[name] * factor).astype(out[name].dtype)
    return out
```

```python
import math
from contextlib import ExitStack

import numpy as np

import concourse.bass as bass
from concourse import mybir

F32 = mybir.dt.float32
I32 = mybir.dt.int32
U32 = mybir.dt.uint32
U8 = mybir.dt.uint8
ALU = mybir.AluOpType
ACT = mybir.ActivationFunctionType
AX = mybir.AxisListType

P = 128
D = 1024
KC = D // P
SEQ = 512
DEPTH = 2
NB = SEQ // P
STEPS = DEPTH * NB
EPS = 1e-6

GM_HEADS, GM_DIM = 4, 64
GM_W = GM_HEADS * GM_DIM
AH, NOPE, ROPE, VD = 8, 64, 32, 64
QK = NOPE + ROPE
QR, KVR = 256, 128
HALF = ROPE // 2
ATT_SCALE = float(QK) ** -0.5
MASKED = -1e30
HP = 2
HG_W = 256
GATE_FLOOR = 1e-20
LEVELS = [64, 32, 16, 8, 4, 2, 1]
NL = len(LEVELS)
EXP_CAP = 80.0
GELU_C = -2.0 * math.sqrt(2.0 / math.pi)
GELU_A = 0.044715
LN_SHIFT = 16.0

IN_W = 2 * GM_W + QR + KVR + ROPE + 4 * HG_W
C_HQ = 2 * GM_W + QR + KVR + ROPE
C_HI = C_HQ + 2 * HG_W
TOKW = C_HQ

PH, NK, TK = 8, 128, 16
SLOTS = PH * TK
GR = 8
NG = SLOTS // GR
TURN = 4
VR = 4

G_MIX, G_Y, G_Q, G_KV, G_B, G_LB, G_OM = 0, 8, 16, 18, 19, 23, 25
GN = 27
ROWS = 25

RING = 3
CH_GM, CH_UQ, CH_UKV, CH_WO, CH_WQ, CH_SK = 0, 1, 3, 4, 12, 20
NCH = 21


def build(nc, x, positions, norm_mix, w_in, gm_v_norm, gm_ws, gm_b, gm_out_norm, mla_q_norm, mla_w_uq,
          mla_kv_norm, mla_w_ukv, mla_out_norm, hg_lb_logits, hg_out_norm, w_out, norm_ffn, peer_w_q,
          peer_sub_keys, peer_u, peer_v, norm_final, out):
    ctx = ExitStack()

    def sb(name, shape, dt=F32):
        return ctx.enter_context(nc.sbuf_tensor(name, shape, dt))

    def sem(name):
        return ctx.enter_context(nc.semaphore(name))

    with ctx:
        x_work = nc.dram_tensor("x_work", (NB, P, D), F32, kind="Internal").ap()
        x_blocks = x[0].rearrange("(b p) d -> b p d", p=P)
        out_blocks = out[0].rearrange("(b p) d -> b p d", p=P)

        win = sb("win", [P, KC, IN_W])
        ring = sb("ring", [P, RING, D])
        u_rows = sb("u_rows", [P, GR, D])
        v_rows = sb("v_rows", [P, VR, D])
        diag = sb("diag", [P, GR, P])
        ids = sb("ids", [P, TURN, GR], U32)
        ids_ring = sb("ids_ring", [P, 2 * SLOTS], U32)
        gates_next = sb("gates_next", [P, SLOTS])
        gates_cur = sb("gates_cur", [P, SLOTS])
        xn_cur = sb("xn_cur", [P, D])
        hid = sb("hid", [P, GR])
        hid_e = sb("hid_e", [P, GR])
        hid_w = sb("hid_w", [P, GR])
        x_cur = sb("x_cur", [P, D])
        feat = sb("feat", [P, D])
        nT = sb("nT", [P, KC, P])
        qT = sb("qT", [P, D])
        k_cache = sb("k_cache", [QK, AH, SEQ])
        v_cache = sb("v_cache", [P, NB, AH * VD])
        ig = sb("ig", [P, 2 * HG_W])
        qf = sb("qf", [P, 2 * HP, P])
        state = sb("state", [P, HP, P])
        ident = sb("ident", [P, P])
        tri = sb("tri", [P, P])
        causal = sb("causal", [P, SEQ + 3 * P])
        pair_mask = sb("pair_mask", [P, NL + 1, P], U8)
        ones = sb("ones", [P, P])
        iota16 = sb("iota16", [P, TK])
        keep = sb("keep", [P, NB])

        gains = sb("gains", [P, DEPTH, GN])
        gcur = sb("gcur", [P, GN])
        gvn = sb("gvn", [P, GM_W])
        rope_tab = sb("rope_tab", [P, NB, ROPE])
        rope_cur = sb("rope_cur", [P, ROPE])
        pos_i = sb("pos_i", [P, NB], I32)
        small = sb("small", [P, 64])
        SCR = 5888
        scr = sb("scr", [P, SCR])

        def part(at, n):
            return scr[:, at:at + n]

        rows = scr[0:DEPTH * ROWS, 512:512 + P]
        uvc = part(0, TOKW)
        gl = part(928, 512)
        cn = part(1440, 384)
        cT = part(1824, 384)
        qs = part(2208, AH * QK)
        kf = part(2976, AH * QK)
        rt = part(3744, 4 * P)
        kr = part(4256, 5 * ROPE)
        gmT = part(4416, 512)
        e4 = part(0, 4 * HG_W)
        wl = part(1024, 9 * HG_W)
        hq = part(3328, HG_W)
        hk = part(3584, HG_W)
        q_l = part(3840, 2 * HG_W)
        k_l = part(4352, 2 * HG_W)
        aT = part(4864, 4 * P)
        kd = part(5376, HG_W)
        kdT = part(5632, HG_W)
        o_sb = e4[:, 0:HG_W]
        o_sq = e4[:, HG_W:2 * HG_W]
        sc = part(0, 2 * SEQ)
        pT = part(1024, 2 * SEQ)
        y_sq = part(2048, AH * VD)
        x_sq = part(0, D)
        qpT = part(0, D)
        subT = part(1024, D)
        ks = part(2048, 2 * 2 * NK)
        ks2 = part(2560, NK)
        top = part(2688, 2 * TK)
        topi = part(2720, 2 * TK)
        cand = part(2752, TK * TK)
        best = part(3264, SLOTS)
        posf = part(3392, 2 * TK)
        hot = part(3424, TK * TK)
        picked = part(3680, 2 * TK)
        idf = part(3712, SLOTS)
        gsum = part(3840, 2 * PH)
        topu = part(3856, 2 * TK).bitcast(U32)
        posu = part(3888, 3 * TK).bitcast(U32)

        bank = ctx.enter_context(nc.psum_tensor("bank", [P, 6, 512], F32))
        vsum = ctx.enter_context(nc.psum_tensor("vsum", [P, D], F32))

        def banks(a, n):
            return bank[:, a:a + n, :].rearrange("p a n -> p (a n)")

        consts = sem("consts")
        passed = sem("passed")
        rows_in, pos_in, win_in = sem("rows_in"), sem("pos_in"), sem("win_in")
        gains_ready, tables_ready = sem("gains_ready"), sem("tables_ready")
        lb_arg, lb_exp, rope_arg = sem("lb_arg"), sem("lb_exp"), sem("rope_arg")
        rowsT = sem("rowsT")
        x_init = sem("x_init")
        x_in, x_stored, x_new, x_taken = sem("x_in"), sem("x_stored"), sem("x_new"), sem("x_taken")
        gvn_in, gain_in = sem("gvn_in"), sem("gain_in")
        chunk_in = [sem(f"chunk_in{i}") for i in range(RING)]
        chunk_free = sem("chunk_free")
        norm_ready, normT, nT_ready, proj, proj_out = (sem(n) for n in (
            "norm_ready", "normT", "nT_ready", "proj", "proj_out"))
        gmT_ready, gelu_arg, gelu_exp, vhat, z_ps = (sem(n) for n in (
            "gmT_ready", "gelu_arg", "gelu_exp", "vhat", "z_ps"))
        lat_ready, latT, latT_ready, qkv_out, roped, qkT_ps, qkT_ready = (sem(n) for n in (
            "lat_ready", "latT", "latT_ready", "qkv_out", "roped", "qkT_ps", "qkT_ready"))
        hg_arg, hg_exp, f_ready, lnf, dist, decay = (sem(n) for n in (
            "hg_arg", "hg_exp", "f_ready", "lnf", "dist", "decay"))
        level_ready = sem("level_ready")
        level_ps, level_used = sem("level_ps"), sem("level_used")
        kd_ready, kdT_ps, kdT_ready, o_ps, c_done = (sem(n) for n in (
            "kd_ready", "kdT_ps", "kdT_ready", "o_ps", "c_done"))
        s_ps, s_max, p_ready, pT_ps, pT_ready, att_ps, att_out = (sem(n) for n in (
            "s_ps", "s_max", "p_ready", "pT_ps", "pT_ready", "att_ps", "att_out"))
        y_ready, yT_ps, yT_ready, xn_ready, xnT_ps, xnT_ready = (sem(n) for n in (
            "y_ready", "yT_ps", "yT_ready", "xn_ready", "xnT_ps", "xnT_ready"))
        qp_ready, skT_ready, keys_ps = sem("qp_ready"), sem("skT_ready"), sem("keys_ps")
        ks_ready, ks_used = sem("ks_ready"), sem("ks_used")
        sm_arg, sm_exp, ids_ready = sem("sm_arg"), sem("sm_exp"), sem("ids_ready")
        u_in = [sem(f"u_in{j}") for j in range(GR)]
        v_in = [sem(f"v_in{j}") for j in range(VR)]
        u_free, v_free = sem("u_free"), sem("v_free")
        hid_arg, hid_exp, w_ready, diag_ready = (sem(n) for n in (
            "hid_arg", "hid_exp", "w_ready", "diag_ready"))
        handed, fin_in, fin_ready, fin_out, gainf_in = (sem(n) for n in (
            "handed", "fin_in", "fin_ready", "fin_out", "gainf_in"))

        def await_(eng, s_, value):
            eng.wait_ge(s_, value)
            if not isinstance(value, int):
                eng.sem_inc(passed, 1)

        def used(s, c):
            return NCH * s + RING + c + 1

        block = ctx.enter_context(nc.Block())

        @block.sync
        def _(sp):
            def load_win(layer):
                sp.dma_start(win[:], w_in[layer].rearrange("(k p) n -> p k n", p=P)).then_inc(win_in, 16)

            def chunk(s, c, dst, src):
                await_(sp, chunk_free, NCH * s + c + 1)
                sp.dma_start(dst, src).then_inc(chunk_in[c % RING], 16)

            def step(s, layer, prefetch=False):
                b = s - NB * layer
                if not isinstance(s, int) or s > 0:
                    await_(sp, x_taken, s)
                    if layer == 0:
                        sp.wait_ge(x_init, 16)
                    else:
                        await_(sp, x_stored, 16 * (s - NB + 1))
                    await_(sp, c_done, s)
                sp.dma_start(x_cur[:], x_work[b] if not (isinstance(s, int) and s == 0) else x_blocks[0]
                             ).then_inc(x_in, 16)
                sp.dma_start(gvn[:], gm_v_norm[layer:layer + 1, :].to_broadcast([P, GM_W])).then_inc(gvn_in, 16)
                if isinstance(s, int) and s == 0:
                    load_win(0)
                slot = lambda c: ring[:, c % RING, :]
                chunk(s, CH_GM, slot(CH_GM)[:, 0:GM_HEADS * P].rearrange("p (h n) -> p h n", h=GM_HEADS),
                      gm_ws[layer].rearrange("h t s -> t h s"))
                for k in range(2):
                    chunk(s, CH_UQ + k, slot(CH_UQ + k)[:, 0:AH * QK], mla_w_uq[layer, k * P:(k + 1) * P, :])
                chunk(s, CH_UKV, slot(CH_UKV), mla_w_ukv[layer])
                if prefetch:
                    await_(sp, proj, s + 1)
                    load_win(layer + 1)
                for k in range(KC):
                    chunk(s, CH_WO + k, slot(CH_WO + k), w_out[layer, k * P:(k + 1) * P, :])
                    if k == RING - 1:
                        await_(sp, s_ps, AH * (s + 1))
                        sp.dma_start(qT[:], norm_ffn[layer:layer + 1, :].to_broadcast([P, D])
                                     ).then_inc(gain_in, 16)
                wq = peer_w_q[layer].rearrange("(k p) (h n) -> h p k n", p=P, h=PH)
                for h in range(PH):
                    chunk(s, CH_WQ + h, slot(CH_WQ + h).rearrange("p (k n) -> p k n", k=KC), wq[h])
                chunk(s, CH_SK, slot(CH_SK).rearrange("p (a n) -> p a n", a=2 * PH),
                      peer_sub_keys[layer].rearrange("h c k n -> k (h c) n"))
                if not isinstance(s, int) or s > 0:
                    await_(sp, x_new, s)
                    sp.dma_start(x_work[(s - 1) % NB], nT[:].rearrange("p k n -> p (k n)")
                                 ).then_inc(x_stored, 16)

            for layer in range(DEPTH):
                r = layer * ROWS
                for src, n in ((norm_mix, 8), (gm_out_norm, 2), (mla_out_norm, 4), (hg_out_norm, 2),
                               (mla_q_norm, 2), (mla_kv_norm, 1)):
                    sp.dma_start(rows[r:r + n, :], src[layer].rearrange("(c p) -> c p", p=P)
                                 ).then_inc(rows_in, 16)
                    r += n
                sp.dma_start(rows[r:r + 4, :], gm_b[layer]).then_inc(rows_in, 16)
                sp.dma_start(rows[r + 4:r + 6, :], hg_lb_logits[layer].rearrange("(c p) -> c p", p=P)
                             ).then_inc(rows_in, 16)
            sp.dma_start(pos_i[:], positions.rearrange("a (b p) -> p (a b)", p=P),
                         allow_slow_non_contiguous=True).then_inc(pos_in, 16)
            sp.wait_ge(consts, 3)
            step(0, 0)
            sp.dma_start(x_work[:], x_blocks).then_inc(x_init, 16)
            with sp.Fori(1, NB - 1) as s:
                step(s, 0)
            step(NB - 1, 0, prefetch=True)
            with sp.Fori(NB, STEPS) as s:
                step(s, 1)
            sp.wait_ge(xn_ready, STEPS)
            sp.dma_start(qT[:], norm_final.rearrange("(a n) -> a n", a=1).to_broadcast([P, D])
                         ).then_inc(gainf_in, 16)
            sp.wait_ge(x_taken, STEPS)
            sp.wait_ge(x_stored, 16 * (STEPS - 1))
            for b in range(NB):
                if b < NB - 1:
                    if b:
                        sp.wait_ge(fin_ready, b)
                    sp.dma_start(x_cur[:], x_work[b]).then_inc(fin_in, 16)
                sp.wait_ge(fin_ready, b + 1)
                sp.dma_start(out_blocks[b], feat[:]).then_inc(fin_out, 16)
            sp.wait_ge(fin_out, 16 * NB)

        @block.gpsimd
        def _(pool):
            pool.memset(ident[:], 0.0)
            pool.memset(tri[:], 1.0)
            pool.memset(causal[:], 0.0)
            pool.memset(ones[:], 1.0)
            pool.memset(keep[:, 1:NB], 1.0)
            pool.memset(keep[:, 0:1], 0.0)
            pool.memset(state[:], 0.0)
            pool.memset(k_cache[:], 0.0)
            pool.memset(v_cache[:], 0.0)
            pool.iota(iota16[:], [[1, TK]], base=0, channel_multiplier=0,
                      allow_small_or_imprecise_dtypes=True)
            pool.drain()
            pool.affine_select(out=ident[:], in_=ident[:], compare_op=ALU.not_equal, fill=1.0, base=0,
                               pattern=[[-1, P]], channel_multiplier=1).then_inc(consts, 1)
            pool.affine_select(out=tri[:], in_=tri[:], compare_op=ALU.is_ge, fill=0.0, base=0,
                               pattern=[[1, P]], channel_multiplier=-1)
            pool.affine_select(out=causal[:], in_=causal[:], compare_op=ALU.is_ge, fill=MASKED,
                               base=3 * P, pattern=[[-1, SEQ + 3 * P]], channel_multiplier=1).then_inc(consts, 1)
            lm = part(0, P)
            for m, h in enumerate(LEVELS):
                g = P // (2 * h)
                seg = lm.rearrange("p (g r) -> p g r", r=2 * h)
                pool.memset(lm, 0.0)
                pool.drain()
                pool.memset(seg[:, :, h:2 * h], 1.0)
                pool.drain()
                pool.affine_select(out=seg, in_=seg, compare_op=ALU.is_ge, fill=0.0, base=0,
                                   pattern=[[-2 * h, g], [0, 2 * h]], channel_multiplier=1)
                pool.drain()
                pool.affine_select(out=seg, in_=seg, compare_op=ALU.is_ge, fill=0.0, base=h - 1,
                                   pattern=[[2 * h, g], [0, 2 * h]], channel_multiplier=-1)
                pool.drain()
                pool.tensor_copy(pair_mask[:, m, :], lm)
                pool.drain()
            pool.tensor_copy(pair_mask[:, NL, :], ident[:]).then_inc(consts, 1)
            pool.wait_ge(consts, 3)

            def take_ids(g, q, fresh=False):
                if not fresh:
                    await_(pool, diag_ready, g - TURN + 2)
                await_(pool, ids_ready, g // NG + 1)
                nc.gpsimd.tensor_copy(ids[:, q, :], ids_ring[:, bass.ds(GR * (g % (2 * NG)), GR)])
                pool.drain()

            def gather_u(g, q, j):
                await_(pool, u_free, GR * g + j + 1)
                pool.indirect_dma_start(u_rows[:, j, :], None, u_tab,
                                        bass.IndirectOffsetOnAxis(ids[:, q, j:j + 1], 0)).then_inc(u_in[j], 16)

            def gather_v(g, q, j):
                await_(pool, v_free, GR * g + j + 1)
                pool.indirect_dma_start(v_rows[:, j % VR, :], None, v_tab,
                                        bass.IndirectOffsetOnAxis(ids[:, q, j:j + 1], 0)).then_inc(v_in[j % VR], 16)

            u_tab = peer_u.rearrange("l e d -> (l e) d")
            v_tab = peer_v.rearrange("l e d -> (l e) d")

            def turn(g, first=False, last=False):
                for q in range(TURN):
                    more = not (last and q == TURN - 1)
                    nq = (q + 1) % TURN
                    if more:
                        take_ids(g + q + 1, nq, fresh=first and nq > 0)
                    for j in range(GR):
                        gather_v(g + q, q, j)
                        if more:
                            gather_u(g + q + 1, nq, j)

            take_ids(0, 0, fresh=True)
            for j in range(GR):
                gather_u(0, 0, j)
            turn(0, first=True)
            with pool.Fori(TURN, STEPS * NG - TURN, TURN) as g:
                turn(g)
            turn(STEPS * NG - TURN, last=True)

        @block.vector
        def _(dve):
            v = nc.vector

            def rsqrt(var, n, y, t):
                yi = y.bitcast(I32)
                v.tensor_scalar(yi, var.bitcast(I32), -0.5, 1597463007.0, ALU.mult, ALU.add)
                dve.drain()
                for _ in range(3):
                    v.tensor_tensor(t, y, var, ALU.mult)
                    dve.drain()
                    v.scalar_tensor_tensor(t, t, -0.5, y, ALU.mult, ALU.mult)
                    dve.drain()
                    v.scalar_tensor_tensor(y, t, 1.5, y, ALU.add, ALU.mult)
                    dve.drain()

            def row_rstd(src, sq, width):
                v.tensor_tensor_reduce(out=sq, in0=src, in1=src, scale=1.0, scalar=0.0, op0=ALU.mult,
                                       op1=ALU.add, accum_out=small[:, 0:1])
                dve.drain()
                v.tensor_scalar(small[:, 0:1], small[:, 0:1], 1.0 / width, EPS, ALU.mult, ALU.add)
                dve.drain()
                rsqrt(small[:, 0:1], 1, small[:, 1:2], small[:, 2:3])

            def head_rstd(src, sq, n, width):
                v.tensor_tensor(sq, src, src, ALU.mult)
                dve.drain()
                v.tensor_reduce(small[:, 8:8 + n], sq.rearrange("p (h d) -> p h d", h=n), AX.X, ALU.add)
                dve.drain()
                v.tensor_scalar(small[:, 8:8 + n], small[:, 8:8 + n], 1.0 / width, EPS, ALU.mult, ALU.add)
                dve.drain()
                rsqrt(small[:, 8:8 + n], n, small[:, 16:16 + n], small[:, 24:24 + n])

            def heads(ap, n):
                return ap.rearrange("p (h d) -> p h d", h=n)

            def per_head(n, width):
                return small[:, 16:16 + n][:, :, None].to_broadcast([P, n, width])

            def experts(g, i):
                for j in range(GR):
                    dve.wait_ge(u_in[j], 16 * (g + 1))
                    v.tensor_tensor_reduce(out=u_rows[:, j, :], in0=u_rows[:, j, :], in1=xn_cur[:], scale=1.0,
                                           scalar=0.0, op0=ALU.mult, op1=ALU.add,
                                           accum_out=hid[:, j:j + 1]).then_inc(u_free, 1)
                dve.drain()
                v.tensor_tensor(hid_e[:], hid[:], hid[:], ALU.mult)
                dve.drain()
                v.tensor_scalar(hid_e[:], hid_e[:], GELU_A, 1.0, ALU.mult, ALU.add)
                dve.drain()
                v.scalar_tensor_tensor(hid_e[:], hid_e[:], GELU_C, hid[:], ALU.mult, ALU.mult)
                dve.drain()
                v.tensor_scalar(hid_e[:], hid_e[:], EXP_CAP, None, ALU.min).then_inc(hid_arg, 1)
                v.tensor_tensor(hid[:], hid[:], gates_cur[:, bass.ds(GR * i, GR)], ALU.mult)
                dve.wait_ge(hid_exp, g + 1)
                v.tensor_scalar(hid_e[:], hid_e[:], 1.0, None, ALU.add)
                dve.drain()
                v.reciprocal(hid_e[:], hid_e[:])
                dve.drain()
                await_(dve, diag_ready, g)
                v.tensor_tensor(hid_w[:], hid_e[:], hid[:], ALU.mult).then_inc(w_ready, 1)
                dve.drain()

            def front(s, body):
                first = isinstance(s, int)
                b = s % NB
                layer = s // NB
                body(0)
                await_(dve, x_in, 16 * (s + 1))
                v.tensor_copy(gcur[:], gains[:, layer, :] if first else gains[:].rearrange(
                    "p l g -> p (l g)")[:, bass.ds(GN * layer, GN)])
                v.tensor_copy(rope_cur[:], rope_tab[:].rearrange("p b r -> p (b r)")[:, bass.ds(ROPE * b, ROPE)])
                v.tensor_scalar(state[:].rearrange("p a n -> p (a n)"), state[:].rearrange("p a n -> p (a n)"),
                                keep[:, bass.ds(b, 1)], None, ALU.mult)
                row_rstd(x_cur[:], feat[:], D)
                v.tensor_scalar(feat[:], x_cur[:], small[:, 1:2], None, ALU.mult).then_inc(norm_ready, 1)
                await_(dve, normT, s + 1)
                if not first:
                    await_(dve, x_stored, 16 * (s - 1))
                v.tensor_tensor(nT[:], banks(0, 2).rearrange("p (k n) -> p k n", k=KC),
                                gcur[:, G_MIX:G_MIX + KC][:, :, None].to_broadcast([P, KC, P]),
                                ALU.mult).then_inc(nT_ready, 1)
                body(1)
                await_(dve, proj_out, s + 1)
                await_(dve, chunk_free, used(s, CH_GM))
                v.tensor_tensor(heads(gmT, GM_HEADS), heads(banks(0, 1), GM_HEADS),
                                tri[:, None, :].to_broadcast([P, GM_HEADS, P]), ALU.mult).then_inc(gmT_ready, 1)
                uv = uvc[:, 0:2 * GM_W]
                v.tensor_tensor(gl, uv, uv, ALU.mult)
                dve.drain()
                v.tensor_scalar(gl, gl, GELU_A, 1.0, ALU.mult, ALU.add)
                dve.drain()
                v.scalar_tensor_tensor(gl, gl, GELU_C, uv, ALU.mult, ALU.mult)
                dve.drain()
                v.tensor_scalar(gl, gl, EXP_CAP, None, ALU.min).then_inc(gelu_arg, 1)
                cq = uvc[:, 2 * GM_W:2 * GM_W + QR]
                ckv = uvc[:, 2 * GM_W + QR:2 * GM_W + QR + KVR]
                row_rstd(cq, cn[:, 0:QR], QR)
                v.tensor_scalar(cn[:, 0:QR], cq, small[:, 1:2], None, ALU.mult)
                dve.drain()
                row_rstd(ckv, cn[:, QR:QR + KVR], KVR)
                v.tensor_scalar(cn[:, QR:QR + KVR], ckv, small[:, 1:2], None, ALU.mult).then_inc(lat_ready, 1)
                await_(dve, gelu_exp, s + 1)
                v.tensor_scalar(gl, gl, 1.0, None, ALU.add)
                dve.drain()
                v.reciprocal(gl, gl)
                dve.drain()
                v.tensor_tensor(uv, uv, gl, ALU.mult)
                dve.drain()
                vv = uvc[:, GM_W:2 * GM_W]
                head_rstd(vv, gl[:, 0:GM_W], GM_HEADS, GM_DIM)
                v.tensor_tensor(heads(vv, GM_HEADS), heads(vv, GM_HEADS), per_head(GM_HEADS, GM_DIM),
                                ALU.mult).then_inc(vhat, 1)
                await_(dve, latT, s + 1)
                v.tensor_tensor(heads(cT, 3), heads(banks(2, 1)[:, 0:384], 3),
                                gcur[:, G_Q:G_Q + 3][:, :, None].to_broadcast([P, 3, P]),
                                ALU.mult).then_inc(latT_ready, 1)
                body(2)
                await_(dve, z_ps, s + 1)
                await_(dve, gvn_in, 16 * (s + 1))
                z = gl[:, 0:GM_W]
                v.tensor_tensor(z, banks(1, 1)[:, 0:GM_W], gvn[:], ALU.mult)
                dve.drain()
                v.tensor_tensor(heads(z, GM_HEADS), heads(z, GM_HEADS),
                                gcur[:, G_B:G_B + GM_HEADS][:, :, None].to_broadcast([P, GM_HEADS, GM_DIM]), ALU.add)
                dve.drain()
                v.tensor_tensor(z, z, uvc[:, 0:GM_W], ALU.mult)
                dve.drain()
                head_rstd(z, gl[:, GM_W:2 * GM_W], GM_HEADS, GM_DIM)
                v.tensor_tensor(heads(feat[:, 0:GM_W], GM_HEADS), heads(z, GM_HEADS), per_head(GM_HEADS, GM_DIM),
                                ALU.mult)
                await_(dve, qkv_out, s + 1)
                q3 = qs3 = heads(qs, AH)
                cosq = rope_cur[:, None, 0:HALF].to_broadcast([P, AH, HALF])
                sinq = rope_cur[:, None, HALF:ROPE].to_broadcast([P, AH, HALF])
                t = [heads(rt[:, i * P:(i + 1) * P], AH) for i in range(4)]
                q1, q2 = q3[:, :, NOPE:NOPE + HALF], q3[:, :, NOPE + HALF:QK]
                v.tensor_tensor(t[0], q1, cosq, ALU.mult)
                v.tensor_tensor(t[1], q2, sinq, ALU.mult)
                v.tensor_tensor(t[2], q2, cosq, ALU.mult)
                v.tensor_tensor(t[3], q1, sinq, ALU.mult)
                k1 = uvc[:, TOKW - ROPE:TOKW - HALF]
                k2 = uvc[:, TOKW - HALF:TOKW]
                kt = [kr[:, i * HALF:(i + 1) * HALF] for i in range(6)]
                v.tensor_tensor(kt[0], k1, rope_cur[:, 0:HALF], ALU.mult)
                v.tensor_tensor(kt[1], k2, rope_cur[:, HALF:ROPE], ALU.mult)
                v.tensor_tensor(kt[2], k2, rope_cur[:, 0:HALF], ALU.mult)
                v.tensor_tensor(kt[3], k1, rope_cur[:, HALF:ROPE], ALU.mult)
                dve.drain()
                v.tensor_tensor(qs3[:, :, NOPE:NOPE + HALF], t[0], t[1], ALU.subtract)
                v.tensor_tensor(qs3[:, :, NOPE + HALF:QK], t[2], t[3], ALU.add)
                v.tensor_tensor(kt[4], kt[0], kt[1], ALU.subtract)
                v.tensor_tensor(kt[5], kt[2], kt[3], ALU.add)
                dve.drain()
                v.tensor_copy(heads(kf, AH)[:, :, NOPE:QK],
                              kr[:, None, 4 * HALF:6 * HALF].to_broadcast([P, AH, ROPE])).then_inc(roped, 1)
                body(3)
                await_(dve, qkT_ps, s + 1)
                qf2 = qf[:].rearrange("p a n -> p (a n)")
                v.tensor_scalar(e4[:, 0:2 * HG_W], qf2, -1.0, EXP_CAP, ALU.mult, ALU.min)
                v.tensor_scalar(e4[:, 2 * HG_W:3 * HG_W], qf2[:, HG_W:2 * HG_W], EXP_CAP, None, ALU.min)
                v.tensor_scalar(e4[:, 3 * HG_W:4 * HG_W], ig[:, HG_W:2 * HG_W], -1.0, EXP_CAP, ALU.mult,
                                ALU.min).then_inc(hg_arg, 1)
                v.memset(aT, 0.0)
                await_(dve, hg_exp, s + 1)
                v.tensor_scalar(e4, e4, 1.0, None, ALU.add)
                dve.drain()
                v.reciprocal(e4, e4)
                dve.drain()
                v.tensor_tensor(hq, qf2[:, 0:HG_W], e4[:, 0:HG_W], ALU.mult)
                for a in range(HP):
                    at = slice(a * P, (a + 1) * P)
                    v.tensor_scalar(hk[:, at], e4[:, 2 * HG_W:3 * HG_W][:, at], gcur[:, G_OM + a:G_OM + a + 1], None,
                                    ALU.mult)
                    v.tensor_scalar(e4[:, HG_W:2 * HG_W][:, at], e4[:, HG_W:2 * HG_W][:, at],
                                    gcur[:, G_OM + a:G_OM + a + 1], gcur[:, G_LB + a:G_LB + a + 1], ALU.mult, ALU.add)
                v.tensor_tensor(ig[:, HG_W:2 * HG_W], ig[:, HG_W:2 * HG_W], e4[:, 3 * HG_W:4 * HG_W], ALU.mult)
                dve.drain()
                lf = e4[:, HG_W:2 * HG_W]
                v.tensor_scalar(lf, lf, GATE_FLOOR, None, ALU.max).then_inc(f_ready, 1)
                await_(dve, lnf, s + 1)
                v.tensor_scalar(lf, lf, -math.log(LN_SHIFT), None, ALU.add)
                dve.drain()
                cum = wl[:, 8 * HG_W:9 * HG_W]
                for a in range(HP):
                    v.tensor_tensor_scan(cum[:, a * P:(a + 1) * P], ones[:], lf[:, a * P:(a + 1) * P], 0.0,
                                         ALU.mult, ALU.add)
                dve.drain()
                for m, h in enumerate(LEVELS):
                    c4 = cum.rearrange("p (g r) -> p g r", r=2 * h)
                    v.tensor_tensor(wl[:, m * HG_W:(m + 1) * HG_W].rearrange("p (g r) -> p g r", r=2 * h), c4,
                                    c4[:, :, h - 1:h].to_broadcast([P, HG_W // (2 * h), 2 * h]), ALU.subtract)
                c3 = heads(cum, HP)
                v.tensor_tensor(heads(wl[:, 7 * HG_W:8 * HG_W], HP), c3, c3[:, :, P - 1:P].to_broadcast([P, HP, P]),
                                ALU.subtract).then_inc(dist, 1)
                body(4)
                await_(dve, decay, s + 1)
                v.tensor_tensor(kd, hk, wl[:, 7 * HG_W:8 * HG_W], ALU.mult).then_inc(kd_ready, 1)

                def keep_level(m):
                    await_(dve, level_ps, (NL + 1) * s + m + 1)
                    e = m % 2
                    v.copy_predicated(aT.rearrange("p (x a n) -> p x a n", x=2, a=HP),
                                      pair_mask[:, m, :][:, None, None, :].to_broadcast([P, 2, HP, P]),
                                      bank[:, 2 + 2 * e:4 + 2 * e, 0:HP * P].rearrange("p x (a n) -> p x a n", a=HP)
                                      ).then_inc(level_used, 1)
                    dve.drain()

                for m in range(NL):
                    e = m % 2
                    w = wl[:, m * HG_W:(m + 1) * HG_W]
                    if m >= 2:
                        keep_level(m - 2)
                    v.tensor_tensor(q_l[:, e * HG_W:(e + 1) * HG_W], hq, w, ALU.mult)
                    v.tensor_tensor(k_l[:, e * HG_W:(e + 1) * HG_W], hk, w, ALU.mult).then_inc(level_ready, 1)
                for m in (NL - 2, NL - 1, NL):
                    keep_level(m)
                v.tensor_tensor(q_l[:, 0:HG_W], hq, wl[:, 8 * HG_W:9 * HG_W], ALU.mult).then_inc(c_done, 1)
                await_(dve, o_ps, s + 1)
                for a in range(HP):
                    for e in range(2):
                        r = slice(64 * e, 64 * e + 64)
                        v.scalar_tensor_tensor(state[r, a, r], state[r, a, r],
                                               wl[r, 8 * HG_W + a * P + P - 1:8 * HG_W + a * P + P],
                                               bank[r, 0, HG_W + a * P + 64 * e:HG_W + a * P + 64 * e + 64],
                                               ALU.mult, ALU.add)
                v.tensor_copy(o_sb, banks(0, 1)[:, 0:HG_W])
                dve.drain()
                head_rstd(o_sb, o_sq, 4, 64)
                v.tensor_tensor(heads(o_sb, 4), heads(o_sb, 4), per_head(4, 64), ALU.mult)
                dve.drain()
                v.tensor_tensor(feat[:, 768:1024], o_sb, ig[:, HG_W:2 * HG_W], ALU.mult)
                dve.drain()
                body(5)

                def attend(hp):
                    for e in range(2):
                        n = AH * s + 2 * hp + e + 1
                        se = sc[:, e * SEQ:(e + 1) * SEQ]
                        await_(dve, s_ps, n)
                        v.scalar_tensor_tensor(se, banks(2 + e, 1), ATT_SCALE, causal[:, bass.ds(P * (3 - b), SEQ)],
                                               ALU.mult, ALU.add)
                        dve.drain()
                        v.tensor_reduce(small[:, 34 + e:35 + e], se, AX.X, ALU.max)
                        dve.drain()
                        v.tensor_scalar(small[:, 36 + e:37 + e], small[:, 34 + e:35 + e], -1.0, None,
                                        ALU.mult).then_inc(s_max, 1)
                    body(hp + 6)
                    for e in range(2):
                        n = AH * s + 2 * hp + e + 1
                        await_(dve, att_ps, n)
                        v.reciprocal(small[:, 40 + e:41 + e], small[:, 38 + e:39 + e])
                        dve.drain()
                        v.tensor_scalar(feat[:, bass.ds(256 + 2 * VD * hp + VD * e, VD)], bank[:, e, 0:VD],
                                        small[:, 40 + e:41 + e], None, ALU.mult).then_inc(att_out, 1)
                    dve.drain()

                with dve.Fori(0, AH // 2) as hp:
                    attend(hp)
                head_rstd(feat[:, 256:768], y_sq, AH, VD)
                v.tensor_tensor(heads(feat[:, 256:768], AH), heads(feat[:, 256:768], AH), per_head(AH, VD),
                                ALU.mult).then_inc(y_ready, 1)
                await_(dve, yT_ps, s + 1)
                v.tensor_tensor(nT[:], banks(0, 2).rearrange("p (k n) -> p k n", k=KC),
                                gcur[:, G_Y:G_Y + KC][:, :, None].to_broadcast([P, KC, P]),
                                ALU.mult).then_inc(yT_ready, 1)
                body(10)
                await_(dve, chunk_free, used(s, CH_WO + KC - 1))
                v.tensor_tensor(x_cur[:], x_cur[:], banks(2, 2), ALU.add)
                dve.drain()
                row_rstd(x_cur[:], x_sq, D)
                v.tensor_scalar(feat[:], x_cur[:], small[:, 1:2], None, ALU.mult)
                dve.drain()
                await_(dve, gain_in, 16 * (s + 1))
                v.tensor_tensor(feat[:], feat[:], qT[:], ALU.mult).then_inc(xn_ready, 1)

                def sixteen(src, dst, index, spare, n):
                    for r in range(2):
                        at = src if r == 0 else spare
                        v.max(dst[:, 8 * r:8 * r + 8], at)
                        dve.drain()
                        v.max_index(index[:, 8 * r:8 * r + 8], dst[:, 8 * r:8 * r + 8], at)
                        if r == 0:
                            v.match_replace(spare, dst[:, 0:8], src, -3e38)
                            dve.drain()

                def route(hp):
                    for e in range(2):
                        n = PH * s + 2 * hp + e + 1
                        await_(dve, ks_ready, n)
                        for c in range(2):
                            sixteen(ks[:, (2 * e + c) * NK:(2 * e + c + 1) * NK], top[:, c * TK:(c + 1) * TK],
                                    topu[:, c * TK:(c + 1) * TK], ks2, NK)
                            dve.drain()
                        v.tensor_copy(topi, topu)
                        v.tensor_tensor(cand.rearrange("p (i j) -> p i j", i=TK),
                                        top[:, 0:TK][:, :, None].to_broadcast([P, TK, TK]),
                                        top[:, None, TK:2 * TK].to_broadcast([P, TK, TK]), ALU.add).then_inc(ks_used, 1)
                        dve.drain()
                        sixteen(cand, picked, posu[:, 0:TK], hot, TK * TK)
                        dve.drain()
                        v.tensor_scalar(posu[:, TK:2 * TK], posu[:, 0:TK], 4, None, ALU.logical_shift_right)
                        v.tensor_scalar(posu[:, 2 * TK:3 * TK], posu[:, 0:TK], 15, None, ALU.bitwise_and)
                        v.tensor_copy(best[:, bass.ds(TK * (2 * hp + e), TK)], picked[:, 0:TK])
                        dve.drain()
                        v.tensor_copy(posf, posu[:, TK:3 * TK])
                        dve.drain()
                        for c in range(2):
                            h3 = hot.rearrange("p (k j) -> p k j", k=TK)
                            v.tensor_tensor(h3, posf[:, c * TK:(c + 1) * TK][:, :, None].to_broadcast([P, TK, TK]),
                                            iota16[:, None, :].to_broadcast([P, TK, TK]), ALU.is_equal)
                            dve.drain()
                            v.tensor_tensor(h3, h3, topi[:, None, c * TK:(c + 1) * TK].to_broadcast([P, TK, TK]),
                                            ALU.mult)
                            dve.drain()
                            v.tensor_reduce(picked[:, c * TK:(c + 1) * TK], h3, AX.X, ALU.add)
                            dve.drain()
                        v.scalar_tensor_tensor(idf[:, bass.ds(TK * (2 * hp + e), TK)], picked[:, 0:TK], float(NK),
                                               picked[:, TK:2 * TK], ALU.mult, ALU.add)
                        dve.drain()
                    body(hp + 11)

                with dve.Fori(0, PH // 2) as hp:
                    route(hp)
                v.tensor_scalar(idf, idf, layer_base[:, bass.ds(layer, 1)], None, ALU.add)
                b3 = heads(best, PH)
                g3 = heads(gates_next[:], PH)
                v.tensor_tensor(g3, b3, b3[:, :, 0:1].to_broadcast([P, PH, TK]), ALU.subtract).then_inc(sm_arg, 1)
                dve.drain()
                v.tensor_copy(ids_ring[:, bass.ds(SLOTS * (s % 2), SLOTS)], idf).then_inc(ids_ready, 1)
                await_(dve, sm_exp, s + 1)
                v.tensor_reduce(gsum[:, 0:PH], g3, AX.X, ALU.add)
                dve.drain()
                v.reciprocal(gsum[:, PH:2 * PH], gsum[:, 0:PH])
                dve.drain()
                v.tensor_tensor(g3, g3, gsum[:, PH:2 * PH][:, :, None].to_broadcast([P, PH, TK]), ALU.mult)
                body(15)
                if not first:
                    await_(dve, v_free, VR + SLOTS * s)
                    v.tensor_copy(nT[:].rearrange("p k n -> p (k n)"), vsum[:]).then_inc(x_new, 1)
                dve.drain()
                v.tensor_copy(xn_cur[:], feat[:])
                v.tensor_copy(gates_cur[:], gates_next[:]).then_inc(handed, 1)
                dve.drain()

            layer_base = small[:, 60:62]
            v.memset(small[:], 0.0)
            inv_freq = part(256, HALF)
            freqs = np.exp(np.float32(-math.log(10000.0)) * np.arange(HALF, dtype=np.float32) / np.float32(HALF))
            dve.drain()
            v.memset(small[:, 61:62], float(NK * NK))
            for i in range(HALF):
                v.memset(inv_freq[:, i:i + 1], float(np.float32(freqs[i])))
            posf32 = part(272, NB)
            dve.wait_ge(pos_in, 16)
            v.tensor_copy(posf32, pos_i[:])
            dve.drain()
            ang, turns, red = part(288, NB * HALF), part(352, NB * HALF), part(416, NB * HALF)
            v.tensor_tensor(heads(ang, NB), posf32[:, :, None].to_broadcast([P, NB, HALF]),
                            inv_freq[:, None, :].to_broadcast([P, NB, HALF]), ALU.mult)
            dve.drain()
            two_pi = 2.0 * math.pi
            hi = 6.28125
            mid = float(np.float32(np.round((two_pi - hi) * 2.0 ** 20) / 2.0 ** 20))
            lo = two_pi - hi - mid
            magic = 1.5 * 2.0 ** 23
            for quarter, col in ((0.25, 0), (0.0, HALF)):
                v.tensor_scalar(turns, ang, 1.0 / two_pi, quarter, ALU.mult, ALU.add)
                dve.drain()
                v.tensor_scalar(turns, turns, magic, None, ALU.add)
                dve.drain()
                v.tensor_scalar(turns, turns, -magic, None, ALU.add)
                dve.drain()
                v.scalar_tensor_tensor(red, turns, -hi, ang, ALU.mult, ALU.add)
                dve.drain()
                v.scalar_tensor_tensor(red, turns, -mid, red, ALU.mult, ALU.add)
                dve.drain()
                v.scalar_tensor_tensor(red, turns, -lo, red, ALU.mult, ALU.add)
                dve.drain()
                v.tensor_scalar(red, red, quarter * two_pi, 3.1415925, ALU.add, ALU.min)
                dve.drain()
                v.tensor_scalar(rope_tab[:, :, col:col + HALF], heads(red, NB), -3.1415925, None,
                                ALU.max).then_inc(rope_arg, 1)
                dve.drain()
            dve.wait_ge(rowsT, 1)
            v.tensor_copy(gains[:, :, 0:ROWS], bank[:, 0, 0:DEPTH * ROWS].rearrange("p (l g) -> p l g", l=DEPTH)
                          ).then_inc(gains_ready, 1)
            dve.drain()
            l0, l1 = gains[:, 0, G_LB:G_LB + 2], gains[:, 1, G_LB:G_LB + 2]
            mx, e0, e1, tot = small[:, 44:46], small[:, 46:48], small[:, 48:50], small[:, 50:52]
            v.tensor_tensor(mx, l0, l1, ALU.max)
            dve.drain()
            v.tensor_tensor(e0, l0, mx, ALU.subtract)
            v.tensor_tensor(e1, l1, mx, ALU.subtract).then_inc(lb_arg, 1)
            dve.wait_ge(lb_exp, 1)
            v.tensor_tensor(tot, e0, e1, ALU.add)
            dve.drain()
            v.reciprocal(tot, tot)
            dve.drain()
            v.tensor_tensor(e0, e0, tot, ALU.mult)
            v.tensor_tensor(e1, e1, tot, ALU.mult)
            dve.drain()
            v.tensor_tensor(l0, e0, e0, ALU.subtract)
            v.tensor_tensor(tot, e0, e1, ALU.add)
            dve.drain()
            v.tensor_tensor(l1, tot, e0, ALU.subtract)
            dve.drain()
            v.tensor_scalar(gains[:, :, G_OM:G_OM + 2], gains[:, :, G_LB:G_LB + 2], -1.0, 1.0, ALU.mult, ALU.add)
            dve.drain()
            dve.wait_ge(consts, 3)
            dve.wait_ge(tables_ready, 1)
            front(0, lambda i: None)
            with dve.Fori(1, STEPS) as s:
                front(s, lambda i: experts((s - 1) * NG + i, i))

            def final(b):
                row_rstd(x_cur[:], scr[:, 0:D], D)
                if b:
                    dve.wait_ge(fin_out, 16 * b)
                v.tensor_scalar(feat[:], x_cur[:], small[:, 1:2], None, ALU.mult)
                dve.drain()
                v.tensor_tensor(feat[:], feat[:], qT[:], ALU.mult).then_inc(fin_ready, 1)

            last = (STEPS - 1) * NG
            experts(last, 0)
            dve.wait_ge(gainf_in, 16)
            for b in range(NB - 1):
                dve.wait_ge(fin_in, 16 * (b + 1))
                final(b)
                experts(last + b + 1, b + 1)
            with dve.Fori(NB, NG) as i:
                experts(last + i, i)
            dve.wait_ge(v_free, VR + SLOTS * STEPS)
            v.tensor_copy(x_cur[:], vsum[:])
            dve.drain()
            final(NB - 1)

        @block.scalar
        def _(act):
            a_ = nc.scalar

            def experts(g, i):
                act.wait_ge(hid_arg, g + 1)
                a_.activation(hid_e[:], hid_e[:], ACT.Exp).then_inc(hid_exp, 1)
                act.wait_ge(w_ready, g + 1)
                await_(act, v_free, GR * g + VR)
                for j in range(GR):
                    ins = a_.activation(diag[:, j, :], ident[:], ACT.Copy, scale=hid_w[:, j:j + 1])
                ins.then_inc(diag_ready, 1)

            def front(s, body):
                b = s % NB
                body(0)
                body(1)
                await_(act, proj, s + 1)
                a_.activation(uvc, banks(2, 2)[:, 0:TOKW], ACT.Copy)
                a_.activation(ig[:], banks(4, 1), ACT.Copy)
                a_.activation(qf[:].rearrange("p a n -> p (a n)"), banks(5, 1), ACT.Copy).then_inc(proj_out, 1)
                await_(act, gelu_arg, s + 1)
                a_.activation(gl, gl, ACT.Exp).then_inc(gelu_exp, 1)
                body(2)
                await_(act, chunk_free, used(s, CH_UKV))
                a_.activation(qs, banks(4, 2)[:, 0:AH * QK], ACT.Copy)
                kv = banks(2, 2).rearrange("p (h d) -> p h d", h=AH)
                a_.activation(kf.rearrange("p (h d) -> p h d", h=AH)[:, :, 0:NOPE], kv[:, :, 0:NOPE], ACT.Copy)
                a_.activation(v_cache[:].rearrange("p b n -> p (b n)")[:, bass.ds(AH * VD * b, AH * VD)].rearrange(
                    "p (h d) -> p h d", h=AH), kv[:, :, NOPE:NOPE + VD], ACT.Copy).then_inc(qkv_out, 1)
                body(3)
                await_(act, qkT_ps, s + 1)
                a_.activation(qT[0:QK, :], banks(0, 2)[0:QK, :], ACT.Copy)
                a_.activation(k_cache[:, :, bass.ds(P * b, P)],
                              banks(4, 2)[0:QK, :].rearrange("p (h n) -> p h n", h=AH), ACT.Copy).then_inc(qkT_ready, 1)
                await_(act, hg_arg, s + 1)
                a_.activation(e4, e4, ACT.Exp).then_inc(hg_exp, 1)
                await_(act, f_ready, s + 1)
                lf = e4[:, HG_W:2 * HG_W]
                a_.activation(lf, lf, ACT.Ln, scale=LN_SHIFT).then_inc(lnf, 1)
                body(4)
                await_(act, dist, s + 1)
                a_.activation(wl, wl, ACT.Abs)
                act.drain()
                a_.activation(wl, wl, ACT.Exp, scale=-1.0).then_inc(decay, 1)
                await_(act, kdT_ps, s + 1)
                a_.activation(kdT, banks(1, 1)[:, 0:HG_W], ACT.Copy).then_inc(kdT_ready, 1)
                body(5)

                def attend(hp):
                    for e in range(2):
                        se = sc[:, e * SEQ:(e + 1) * SEQ]
                        await_(act, s_max, AH * s + 2 * hp + e + 1)
                        a_.activation(se, se, ACT.Exp, bias=small[:, 36 + e:37 + e],
                                      accum_out=small[:, 38 + e:39 + e]).then_inc(p_ready, 1)
                    for e in range(2):
                        await_(act, pT_ps, AH * s + 2 * hp + e + 1)
                        a_.activation(pT[:, e * SEQ:(e + 1) * SEQ], banks(4 + e, 1), ACT.Copy).then_inc(pT_ready, 1)
                    body(hp + 6)

                with act.Fori(0, AH // 2) as hp:
                    attend(hp)
                body(10)
                await_(act, xnT_ps, s + 1)
                a_.activation(nT[:].rearrange("p k n -> p (k n)"), banks(0, 2), ACT.Copy).then_inc(xnT_ready, 1)
                await_(act, chunk_free, used(s, CH_WQ + PH - 1))
                a_.activation(qpT, banks(4, 2), ACT.Copy).then_inc(qp_ready, 1)
                await_(act, chunk_free, used(s, CH_SK))
                a_.activation(subT, banks(2, 2), ACT.Copy).then_inc(skT_ready, 1)

                def route(hp):
                    for e in range(2):
                        await_(act, ks_used, PH * s + 2 * hp)
                        if e == 0:
                            await_(act, keys_ps, s + 1)
                        a_.activation(ks[:, e * 2 * NK:(e + 1) * 2 * NK].rearrange("p (c n) -> p c n", c=2),
                                      banks(0, 4).rearrange("p (c n) -> p c n", c=2)[:, :, bass.ds(NK * (2 * hp + e), NK)],
                                      ACT.Copy
                                      ).then_inc(ks_ready, 1)
                    body(hp + 11)

                with act.Fori(0, PH // 2) as hp:
                    route(hp)
                await_(act, sm_arg, s + 1)
                a_.activation(gates_next[:], gates_next[:], ACT.Exp).then_inc(sm_exp, 1)
                body(15)

            act.wait_ge(rope_arg, 2)
            rt_all = rope_tab[:].rearrange("p b r -> p (b r)")
            a_.activation(rt_all, rt_all, ACT.Sin).then_inc(tables_ready, 1)
            act.wait_ge(lb_arg, 1)
            a_.activation(small[:, 46:50], small[:, 46:50], ACT.Exp).then_inc(lb_exp, 1)
            act.wait_ge(consts, 3)
            front(0, lambda i: None)
            with act.Fori(1, STEPS) as s:
                front(s, lambda i: experts((s - 1) * NG + i, i))
            last = (STEPS - 1) * NG
            with act.Fori(0, NG) as i:
                experts(last + i, i)

        @block.tensor
        def _(pe):
            mm = nc.tensor.matmul

            def transposes(dst, src, n, width):
                for k in range(n):
                    last = nc.tensor.transpose(dst[0:width, k * P:(k + 1) * P], src[:, k * width:(k + 1) * width], ident[:])
                return last

            def chunk(s, c):
                pe.wait_ge(chunk_in[c % RING], 16 * (NCH // RING * s + c // RING + 1))
                return ring[:, c % RING, :]

            def experts(g, i, lead=False):
                pe.wait_ge(diag_ready, g + 1)
                for j in range(GR):
                    pe.wait_ge(v_in[j % VR], 16 * (2 * g + j // VR + 1))
                    for n in range(2):
                        ins = mm(vsum[:, n * 512:(n + 1) * 512], diag[:, j, :], v_rows[:, j % VR, n * 512:(n + 1) * 512],
                                 start=False, stop=False, skip_group_check=True)
                    ins.then_inc(v_free, 1)

            def front(s, body):
                first = isinstance(s, int)
                b = s % NB
                layer = s // NB
                body(0)
                pe.wait_ge(norm_ready, s + 1)
                transposes(banks(0, 2), feat[:], KC, P).then_inc(normT, 1)
                pe.wait_ge(nT_ready, s + 1)
                w = chunk(s, CH_GM)
                last = transposes(banks(0, 1), w, GM_HEADS, P)
                last.then_inc(chunk_free, 1)
                pe.wait_ge(win_in, 16 * (layer + 1))
                for dst, c0, n in ((banks(2, 1), 0, 512), (banks(3, 1), 512, TOKW - 512), (banks(4, 1), C_HI, 512)):
                    for k in range(KC):
                        mm(dst[:, 0:n], nT[:, k, :], win[:, k, c0:c0 + n], start=k == 0, stop=k == KC - 1)
                for a in range(4):
                    for k in range(KC):
                        last = mm(banks(5, 1)[:, a * P:(a + 1) * P], win[:, k, C_HQ + a * P:C_HQ + (a + 1) * P],
                                  nT[:, k, :], start=k == 0, stop=k == KC - 1)
                last.then_inc(proj, 1)
                body(1)
                pe.wait_ge(lat_ready, s + 1)
                pe.wait_ge(proj_out, s + 1)
                transposes(banks(2, 1), cn, 3, P).then_inc(latT, 1)
                pe.wait_ge(gmT_ready, s + 1)
                pe.wait_ge(vhat, s + 1)
                for h in range(GM_HEADS):
                    last = mm(banks(1, 1)[:, h * GM_DIM:(h + 1) * GM_DIM], gmT[:, h * P:(h + 1) * P],
                              uvc[:, GM_W + h * GM_DIM:GM_W + (h + 1) * GM_DIM], start=True, stop=True)
                last.then_inc(z_ps, 1)
                body(2)
                pe.wait_ge(latT_ready, s + 1)
                for k in range(2):
                    w = chunk(s, CH_UQ + k)
                    for c0, n in ((0, 512), (512, 256)):
                        last = mm(banks(4, 2)[:, c0:c0 + n], cT[:, k * P:(k + 1) * P], w[:, c0:c0 + n],
                                  start=k == 0, stop=k == 1)
                    last.then_inc(chunk_free, 1)
                w = chunk(s, CH_UKV)
                for n in range(2):
                    last = mm(banks(2 + n, 1), cT[:, 2 * P:3 * P], w[:, n * 512:(n + 1) * 512], start=True, stop=True)
                last.then_inc(chunk_free, 1)
                pe.wait_ge(qkv_out, s + 1)
                pe.wait_ge(roped, s + 1)
                transposes(banks(0, 2), qs, AH, QK)
                transposes(banks(4, 2), kf, AH, QK).then_inc(qkT_ps, 1)
                body(3)
                body(4)
                pe.wait_ge(kd_ready, s + 1)
                pe.wait_ge(qkT_ready, s + 1)
                transposes(banks(1, 1), kd, HP, P).then_inc(kdT_ps, 1)
                for m in range(NL + 1):
                    e = m % 2
                    if m < NL:
                        pe.wait_ge(level_ready, NL * s + m + 1)
                    if m >= 2:
                        pe.wait_ge(level_used, (NL + 1) * s + m - 1)
                    qq, kk = (q_l[:, e * HG_W:(e + 1) * HG_W], k_l[:, e * HG_W:(e + 1) * HG_W]) if m < NL else (hq, hk)
                    for h in range(4):
                        r = slice(64 * (h % 2), 64 * (h % 2) + 64)
                        c = slice(P * (h // 2), P * (h // 2) + P)
                        last = mm(bank[:, 2 + 2 * e + h % 2, c], kk[r, c], qq[r, c], start=True, stop=True)
                    last.then_inc(level_ps, 1)
                pe.wait_ge(c_done, s + 1)
                pe.wait_ge(kdT_ready, s + 1)
                for a in range(HP):
                    o = banks(0, 1)[:, a * P:(a + 1) * P]
                    mm(o, q_l[:, a * P:(a + 1) * P], state[:, a, :], start=True, stop=False, skip_group_check=True)
                    for e in range(2):
                        mm(o[:, 64 * e:64 * e + 64], aT[:, (2 * e + a) * P:(2 * e + a + 1) * P],
                           ig[:, (2 * a + e) * 64:(2 * a + e + 1) * 64], start=False, stop=True, skip_group_check=True)
                for a in range(HP):
                    last = mm(banks(0, 1)[:, HG_W + a * P:HG_W + (a + 1) * P], kdT[:, a * P:(a + 1) * P],
                              ig[:, a * P:(a + 1) * P], start=True, stop=True)
                last.then_inc(o_ps, 1)
                body(5)

                def attend(hp):
                    pe.wait_ge(s_max, AH * s + 2 * hp)
                    for e in range(2):
                        h = 2 * hp + e
                        mm(banks(2 + e, 1), qT[0:QK, P * h:P * (h + 1)],
                           k_cache[:, h, :],
                           start=True, stop=True).then_inc(s_ps, 1)
                    for e in range(2):
                        pe.wait_ge(p_ready, AH * s + 2 * hp + e + 1)
                        transposes(banks(4 + e, 1), sc[:, e * SEQ:(e + 1) * SEQ], NB, P).then_inc(pT_ps, 1)
                    pe.wait_ge(att_out, AH * s + 2 * hp)
                    for e in range(2):
                        h = 2 * hp + e
                        pe.wait_ge(pT_ready, AH * s + 2 * hp + e + 1)
                        for kb in range(NB):
                            last = mm(bank[:, e, 0:VD], pT[:, e * SEQ + kb * P:e * SEQ + (kb + 1) * P],
                                      v_cache[:, kb, VD * h:VD * (h + 1)], start=kb == 0, stop=kb == NB - 1)
                        last.then_inc(att_ps, 1)
                    body(hp + 6)

                for hp in range(AH // 2):
                    attend(hp)
                pe.wait_ge(y_ready, s + 1)
                transposes(banks(0, 2), feat[:], KC, P).then_inc(yT_ps, 1)
                pe.wait_ge(yT_ready, s + 1)
                for k in range(KC):
                    w = chunk(s, CH_WO + k)
                    for n in range(2):
                        last = mm(banks(2 + n, 1), nT[:, k, :], w[:, n * 512:(n + 1) * 512], start=k == 0,
                                  stop=k == KC - 1, skip_group_check=True)
                    last.then_inc(chunk_free, 1)
                body(10)
                pe.wait_ge(xn_ready, s + 1)
                transposes(banks(0, 2), feat[:], KC, P).then_inc(xnT_ps, 1)
                pe.wait_ge(xnT_ready, s + 1)
                for h in range(PH):
                    w = chunk(s, CH_WQ + h)
                    for k in range(KC):
                        last = mm(banks(4, 2)[:, h * P:(h + 1) * P], w[:, k * P:(k + 1) * P], nT[:, k, :],
                                  start=k == 0, stop=k == KC - 1)
                    last.then_inc(chunk_free, 1)
                w = chunk(s, CH_SK)
                transposes(banks(2, 2), w, PH, P).then_inc(chunk_free, 1)
                pe.wait_ge(qp_ready, s + 1)
                pe.wait_ge(skT_ready, s + 1)
                for h in range(PH):
                    for c in range(2):
                        r = slice(64 * c, 64 * c + 64)
                        last = mm(banks(2 * c, 2)[:, h * NK:(h + 1) * NK], qpT[r, h * P:(h + 1) * P],
                                  subT[r, h * P:(h + 1) * P], start=True, stop=True)
                last.then_inc(keys_ps, 1)
                with pe.Fori(0, PH // 2) as hp:
                    body(hp + 11)
                body(15)
                if not first:
                    pe.wait_ge(x_new, s)
                for n in range(2):
                    last = mm(vsum[:, n * 512:(n + 1) * 512], ident[:], x_cur[:, n * 512:(n + 1) * 512], start=True,
                              stop=False, skip_group_check=True)
                last.then_inc(x_taken, 1)

            pe.wait_ge(rows_in, 16 * 8 * DEPTH)
            pe.wait_ge(consts, 3)
            nc.tensor.transpose(bank[:, 0, 0:DEPTH * ROWS], rows[:], ident[0:DEPTH * ROWS, 0:DEPTH * ROWS]).then_inc(rowsT, 1)
            pe.sem_inc(chunk_free, RING)
            pe.sem_inc(u_free, GR)
            pe.sem_inc(v_free, VR)
            pe.wait_ge(gains_ready, 1)
            front(0, lambda i: None)
            with pe.Fori(1, STEPS) as s:
                front(s, lambda i: experts((s - 1) * NG + i, i))
            last = (STEPS - 1) * NG
            with pe.Fori(0, NG) as i:
                experts(last + i, i)


_INS = ["x", "positions", "norm_mix", "w_in", "gm_v_norm", "gm_ws", "gm_b", "gm_out_norm", "mla_q_norm",
        "mla_w_uq", "mla_kv_norm", "mla_w_ukv", "mla_out_norm", "hg_lb_logits", "hg_out_norm", "w_out",
        "norm_ffn", "peer_w_q", "peer_sub_keys", "peer_u", "peer_v", "norm_final"]


def kernel(**inputs):
    import concourse.bacc as bacc
    from concourse.bass_utils import run_bass_kernel_spmd

    nc = bacc.Bacc("TRN2", target_bir_lowering=False, num_devices=1)
    arrays, args = {}, []
    for name in _INS:
        a = np.ascontiguousarray(inputs[name])
        arrays[f"in_{name}"] = a
        args.append(nc.dram_tensor(f"in_{name}", a.shape, mybir.dt.from_np(a.dtype), kind="ExternalInput").ap())
    out = nc.dram_tensor("out_0", (1, SEQ, D), F32, kind="ExternalOutput").ap()
    build(nc, *args, out)
    r = run_bass_kernel_spmd(nc, [arrays], core_ids=[0])
    return r.results[0]["out_0"]
```

```python
import math
from contextlib import ExitStack

import numpy as np

import concourse.bass as bass
from concourse import mybir

F32 = mybir.dt.float32
I32 = mybir.dt.int32
U32 = mybir.dt.uint32
U8 = mybir.dt.uint8
ALU = mybir.AluOpType
ACT = mybir.ActivationFunctionType
AX = mybir.AxisListType

P = 128
D = 1024
KC = D // P
SEQ = 512
DEPTH = 2
NB = SEQ // P
STEPS = DEPTH * NB
EPS = 1e-6

GM_HEADS, GM_DIM = 4, 64
GM_W = GM_HEADS * GM_DIM
AH, NOPE, ROPE, VD = 8, 64, 32, 64
QK = NOPE + ROPE
QR, KVR = 256, 128
HALF = ROPE // 2
ATT_SCALE = float(QK) ** -0.5
MASKED = -1e30
HP = 2
HG_W = 256
GATE_FLOOR = 1e-20
LEVELS = [64, 32, 16, 8, 4, 2, 1]
NL = len(LEVELS)
EXP_CAP = 80.0
GELU_C = -2.0 * math.sqrt(2.0 / math.pi)
GELU_A = 0.044715
LN_SHIFT = 16.0

IN_W = 2 * GM_W + QR + KVR + ROPE + 4 * HG_W
C_HQ = 2 * GM_W + QR + KVR + ROPE
C_HI = C_HQ + 2 * HG_W
TOKW = C_HQ

PH, NK, TK = 8, 128, 16
SLOTS = PH * TK
GR = 8
NG = SLOTS // GR
TURN = 4
VR = 4
V_START = VR + 1

G_MIX, G_Y, G_Q, G_KV, G_B, G_LB, G_OM = 0, 8, 16, 18, 19, 23, 25
GN = 27
ROWS = 25

RING = 3
CH_GM, CH_UQ, CH_UKV, CH_WO, CH_WQ, CH_SK = 0, 1, 3, 4, 12, 20
NCH = 21


def build(nc, x, positions, norm_mix, w_in, gm_v_norm, gm_ws, gm_b, gm_out_norm, mla_q_norm, mla_w_uq,
          mla_kv_norm, mla_w_ukv, mla_out_norm, hg_lb_logits, hg_out_norm, w_out, norm_ffn, peer_w_q,
          peer_sub_keys, peer_u, peer_v, norm_final, out):
    ctx = ExitStack()

    def sb(name, shape, dt=F32):
        return ctx.enter_context(nc.sbuf_tensor(name, shape, dt))

    def sem(name):
        return ctx.enter_context(nc.semaphore(name))

    with ctx:
        x_work = nc.dram_tensor("x_work", (NB, P, D), F32, kind="Internal").ap()
        x_blocks = x[0].rearrange("(b p) d -> b p d", p=P)
        out_blocks = out[0].rearrange("(b p) d -> b p d", p=P)

        win = sb("win", [P, KC, IN_W])
        ring = sb("ring", [P, RING, D])
        u_rows = sb("u_rows", [P, GR, D])
        v_rows = sb("v_rows", [P, VR, D])
        diag = sb("diag", [P, GR, P])
        ids = sb("ids", [P, TURN, GR], U32)
        ids_ring = sb("ids_ring", [P, 2 * SLOTS], U32)
        gates_next = sb("gates_next", [P, SLOTS])
        gates_cur = sb("gates_cur", [P, SLOTS])
        xn_cur = sb("xn_cur", [P, D])
        hid = sb("hid", [P, GR])
        hid_e = sb("hid_e", [P, GR])
        hid_w = sb("hid_w", [P, GR])
        x_cur = sb("x_cur", [P, D])
        feat = sb("feat", [P, D])
        nT = sb("nT", [P, KC, P])
        qT = sb("qT", [P, D])
        k_cache = sb("k_cache", [QK, AH, SEQ])
        v_cache = sb("v_cache", [P, NB, AH * VD])
        ig = sb("ig", [P, 2 * HG_W])
        qf = sb("qf", [P, 2 * HP, P])
        state = sb("state", [P, HP, P])
        ident = sb("ident", [P, P])
        tri = sb("tri", [P, P])
        causal = sb("causal", [P, SEQ + 3 * P])
        pair_mask = sb("pair_mask", [P, NL + 1, P], U8)
        ones = sb("ones", [P, P])
        iota16 = sb("iota16", [P, TK])
        keep = sb("keep", [P, NB])

        gains = sb("gains", [P, DEPTH, GN])
        gcur = sb("gcur", [P, GN])
        gvn = sb("gvn", [P, GM_W])
        rope_tab = sb("rope_tab", [P, NB, ROPE])
        rope_cur = sb("rope_cur", [P, ROPE])
        pos_i = sb("pos_i", [P, NB], I32)
        small = sb("small", [P, 64])
        SCR = 5888
        scr = sb("scr", [P, SCR])

        def part(at, n):
            return scr[:, at:at + n]

        SETUP = 2 * D
        rows = scr[0:DEPTH * ROWS, SETUP + 512:SETUP + 512 + P]
        x_norm = part(0, D)
        uvc = part(0, TOKW)
        gl = part(928, 512)
        cn = part(1440, 384)
        cT = part(1824, 384)
        qs = part(2208, AH * QK)
        kf = part(2976, AH * QK)
        rt = part(3744, 4 * P)
        kr = part(4256, 5 * ROPE)
        gmT = part(4416, 512)
        e4 = part(0, 4 * HG_W)
        wl = part(1024, 9 * HG_W)
        hq = part(3328, HG_W)
        hk = part(3584, HG_W)
        q_l = part(3840, 2 * HG_W)
        k_l = part(4352, 2 * HG_W)
        aT = part(4864, 4 * P)
        kd = part(5376, HG_W)
        kdT = part(5632, HG_W)
        o_sb = e4[:, 0:HG_W]
        o_sq = e4[:, HG_W:2 * HG_W]
        sc = part(0, 2 * SEQ)
        pT = part(1024, 2 * SEQ)
        y_sq = part(2048, AH * VD)
        x_sq = part(0, D)
        qpT = part(0, D)
        subT = part(1024, D)
        ks = part(2048, 2 * 2 * NK)
        ks2 = part(2560, 2 * 2 * NK)
        hot = part(3072, 4 * TK * TK)
        cand = part(4096, 2 * TK * TK)
        top = part(4608, 4 * TK)
        topi = part(4672, 4 * TK)
        topu = part(4736, 4 * TK).bitcast(U32)
        picked = part(4800, 2 * TK)
        posu = part(4832, 2 * TK).bitcast(U32)
        halfu = part(4864, 4 * TK).bitcast(U32)
        halff = part(4928, 4 * TK)
        chosen = part(4992, 4 * TK)
        best = part(5056, SLOTS)
        idf = part(5184, SLOTS)
        gsum = part(5312, 2 * PH)
        x_rows = part(4864, D)

        bank = ctx.enter_context(nc.psum_tensor("bank", [P, 6, 512], F32))
        vsum = ctx.enter_context(nc.psum_tensor("vsum", [P, D], F32))

        def banks(a, n):
            return bank[:, a:a + n, :].rearrange("p a n -> p (a n)")

        consts = sem("consts")
        passed = sem("passed")
        rows_in, pos_in, win_in = sem("rows_in"), sem("pos_in"), sem("win_in")
        gains_ready, tables_ready = sem("gains_ready"), sem("tables_ready")
        lb_arg, lb_exp, rope_arg = sem("lb_arg"), sem("lb_exp"), sem("rope_arg")
        rowsT = sem("rowsT")
        res_in = sem("res_in")
        x_in, x_stored, x_new, x_taken = sem("x_in"), sem("x_stored"), sem("x_new"), sem("x_taken")
        gvn_in, gain_in = sem("gvn_in"), sem("gain_in")
        chunk_in = [sem(f"chunk_in{i}") for i in range(RING)]
        chunk_free = sem("chunk_free")
        proj_uv, uv_out = sem("proj_uv"), sem("uv_out")
        norm_ready, normT, nT_ready, proj, proj_out = (sem(n) for n in (
            "norm_ready", "normT", "nT_ready", "proj", "proj_out"))
        gmT_ready, gelu_arg, gelu_exp, vhat, z_ps = (sem(n) for n in (
            "gmT_ready", "gelu_arg", "gelu_exp", "vhat", "z_ps"))
        lat_ready, latT, latT_ready, qkv_out, roped, qkT_ps, qkT_ready = (sem(n) for n in (
            "lat_ready", "latT", "latT_ready", "qkv_out", "roped", "qkT_ps", "qkT_ready"))
        hg_arg, hg_exp, f_ready, lnf, dist, decay = (sem(n) for n in (
            "hg_arg", "hg_exp", "f_ready", "lnf", "dist", "decay"))
        level_ready = sem("level_ready")
        level_ps, level_used = sem("level_ps"), sem("level_used")
        kd_ready, kdT_ps, kdT_ready, o_ps, c_done = (sem(n) for n in (
            "kd_ready", "kdT_ps", "kdT_ready", "o_ps", "c_done"))
        s_ps, s_max, p_ready, pT_ps, pT_ready, att_ps, att_out = (sem(n) for n in (
            "s_ps", "s_max", "p_ready", "pT_ps", "pT_ready", "att_ps", "att_out"))
        y_ready, yT_ps, yT_ready, xn_ready, xnT_ps, xnT_ready = (sem(n) for n in (
            "y_ready", "yT_ps", "yT_ready", "xn_ready", "xnT_ps", "xnT_ready"))
        qp_ready, skT_ready, keys_ps = sem("qp_ready"), sem("skT_ready"), sem("keys_ps")
        ks_ready, ks_used = sem("ks_ready"), sem("ks_used")
        sm_arg, sm_exp, ids_ready = sem("sm_arg"), sem("sm_exp"), sem("ids_ready")
        ids_taken = sem("ids_taken")
        u_in = [sem(f"u_in{j}") for j in range(GR)]
        v_in = [sem(f"v_in{j}") for j in range(VR)]
        u_free, v_free = sem("u_free"), sem("v_free")
        hid_arg, hid_exp, w_ready, diag_ready = (sem(n) for n in (
            "hid_arg", "hid_exp", "w_ready", "diag_ready"))
        fin_in, fin_ready, fin_out, gainf_in = (sem(n) for n in (
            "fin_in", "fin_ready", "fin_out", "gainf_in"))

        def await_(eng, s_, value):
            eng.wait_ge(s_, value)
            if not isinstance(value, int):
                eng.sem_inc(passed, 1)

        def used(s, c):
            return NCH * s + RING + c + 1

        block = ctx.enter_context(nc.Block())

        @block.sync
        def _(sp):
            def load_win(layer):
                sp.dma_start(win[:], w_in[layer].rearrange("(k p) n -> p k n", p=P)).then_inc(win_in, 16)

            def chunk(s, c, dst, src):
                await_(sp, chunk_free, NCH * s + c + 1)
                sp.dma_start(dst, src).then_inc(chunk_in[c % RING], 16)

            def step(s, layer, prefetch=False):
                if not isinstance(s, int) or s > 0:
                    await_(sp, c_done, s)
                sp.dma_start(gvn[:], gm_v_norm[layer:layer + 1, :].to_broadcast([P, GM_W])).then_inc(gvn_in, 16)
                slot = lambda c: ring[:, c % RING, :]
                chunk(s, CH_GM, slot(CH_GM)[:, 0:GM_HEADS * P].rearrange("p (h n) -> p h n", h=GM_HEADS),
                      gm_ws[layer].rearrange("h t s -> t h s"))
                for k in range(2):
                    chunk(s, CH_UQ + k, slot(CH_UQ + k)[:, 0:AH * QK], mla_w_uq[layer, k * P:(k + 1) * P, :])
                chunk(s, CH_UKV, slot(CH_UKV), mla_w_ukv[layer])
                if prefetch:
                    await_(sp, proj, s + 1)
                    load_win(layer + 1)
                for k in range(KC):
                    chunk(s, CH_WO + k, slot(CH_WO + k), w_out[layer, k * P:(k + 1) * P, :])
                    if k == RING - 1:
                        await_(sp, s_ps, AH * (s + 1))
                        sp.dma_start(qT[:], norm_ffn[layer:layer + 1, :].to_broadcast([P, D])
                                     ).then_inc(gain_in, 16)
                wq = peer_w_q[layer].rearrange("(k p) (h n) -> h p k n", p=P, h=PH)
                for h in range(PH):
                    chunk(s, CH_WQ + h, slot(CH_WQ + h).rearrange("p (k n) -> p k n", k=KC), wq[h])
                chunk(s, CH_SK, slot(CH_SK).rearrange("p (a n) -> p a n", a=2 * PH),
                      peer_sub_keys[layer].rearrange("h c k n -> k (h c) n"))
                if isinstance(s, int) and s == STEPS - 1:
                    x_next = None
                elif isinstance(s, int) and s == NB - 1 or layer > 0:
                    await_(sp, x_stored, 16 * (s - NB + 3))
                    x_next = x_work[(s + 1) % NB]
                else:
                    x_next = x_blocks[s + 1]
                if x_next is not None:
                    await_(sp, keys_ps, s + 1)
                    sp.dma_start(x_norm, x_next).then_inc(x_in, 16)
                if not isinstance(s, int) or s > 0:
                    await_(sp, x_new, s)
                    sp.dma_start(x_work[(s - 1) % NB], x_rows).then_inc(x_stored, 16)
                if x_next is not None:
                    await_(sp, x_taken, s + 1)
                    sp.dma_start(x_cur[:], x_next).then_inc(res_in, 16)

            sp.sem_inc(x_stored, 16)
            sp.dma_start(x_norm, x_blocks[0]).then_inc(x_in, 16)
            for layer in range(DEPTH):
                r = layer * ROWS
                for src, n in ((norm_mix, 8), (gm_out_norm, 2), (mla_out_norm, 4), (hg_out_norm, 2),
                               (mla_q_norm, 2), (mla_kv_norm, 1)):
                    sp.dma_start(rows[r:r + n, :], src[layer].rearrange("(c p) -> c p", p=P)
                                 ).then_inc(rows_in, 16)
                    r += n
                sp.dma_start(rows[r:r + 4, :], gm_b[layer]).then_inc(rows_in, 16)
                sp.dma_start(rows[r + 4:r + 6, :], hg_lb_logits[layer].rearrange("(c p) -> c p", p=P)
                             ).then_inc(rows_in, 16)
            sp.dma_start(pos_i[:], positions.rearrange("a (b p) -> p (a b)", p=P),
                         allow_slow_non_contiguous=True).then_inc(pos_in, 16)
            load_win(0)
            sp.dma_start(x_cur[:], x_blocks[0]).then_inc(res_in, 16)
            step(0, 0)
            with sp.Fori(1, NB - 1) as s:
                step(s, 0)
            step(NB - 1, 0, prefetch=True)
            with sp.Fori(NB, STEPS - 1) as s:
                step(s, 1)
            step(STEPS - 1, 1)
            sp.wait_ge(xn_ready, STEPS)
            sp.dma_start(qT[:], norm_final.rearrange("(a n) -> a n", a=1).to_broadcast([P, D])
                         ).then_inc(gainf_in, 16)
            sp.wait_ge(x_taken, STEPS)
            sp.wait_ge(x_stored, 16 * STEPS)
            for b in range(NB):
                if b < NB - 1:
                    if b:
                        sp.wait_ge(fin_ready, b)
                    sp.dma_start(x_cur[:], x_work[b]).then_inc(fin_in, 16)
                sp.wait_ge(fin_ready, b + 1)
                sp.dma_start(out_blocks[b], feat[:]).then_inc(fin_out, 16)
            sp.wait_ge(fin_out, 16 * NB)

        @block.gpsimd
        def _(pool):
            pool.memset(ident[:], 0.0)
            pool.memset(tri[:], 1.0)
            pool.memset(causal[:], 0.0)
            pool.memset(ones[:], 1.0)
            pool.memset(keep[:, 1:NB], 1.0)
            pool.memset(keep[:, 0:1], 0.0)
            pool.memset(state[:], 0.0)
            pool.memset(k_cache[:], 0.0)
            pool.memset(v_cache[:], 0.0)
            pool.iota(iota16[:], [[1, TK]], base=0, channel_multiplier=0,
                      allow_small_or_imprecise_dtypes=True)
            pool.drain()
            pool.affine_select(out=ident[:], in_=ident[:], compare_op=ALU.not_equal, fill=1.0, base=0,
                               pattern=[[-1, P]], channel_multiplier=1).then_inc(consts, 1)
            pool.affine_select(out=tri[:], in_=tri[:], compare_op=ALU.is_ge, fill=0.0, base=0,
                               pattern=[[1, P]], channel_multiplier=-1)
            pool.affine_select(out=causal[:], in_=causal[:], compare_op=ALU.is_ge, fill=MASKED,
                               base=3 * P, pattern=[[-1, SEQ + 3 * P]], channel_multiplier=1).then_inc(consts, 1)
            lm = part(SETUP, P)
            for m, h in enumerate(LEVELS):
                g = P // (2 * h)
                seg = lm.rearrange("p (g r) -> p g r", r=2 * h)
                pool.memset(lm, 0.0)
                pool.drain()
                pool.memset(seg[:, :, h:2 * h], 1.0)
                pool.drain()
                pool.affine_select(out=seg, in_=seg, compare_op=ALU.is_ge, fill=0.0, base=0,
                                   pattern=[[-2 * h, g], [0, 2 * h]], channel_multiplier=1)
                pool.drain()
                pool.affine_select(out=seg, in_=seg, compare_op=ALU.is_ge, fill=0.0, base=h - 1,
                                   pattern=[[2 * h, g], [0, 2 * h]], channel_multiplier=-1)
                pool.drain()
                pool.tensor_copy(pair_mask[:, m, :], lm)
                pool.drain()
            pool.tensor_copy(pair_mask[:, NL, :], ident[:]).then_inc(consts, 1)
            pool.wait_ge(consts, 3)

            def take_ids(g, q, fresh=False):
                if not fresh:
                    await_(pool, diag_ready, 2 * (g - TURN) + 5)
                await_(pool, ids_ready, g // NG + 1)
                nc.gpsimd.tensor_copy(ids[:, q, :], ids_ring[:, bass.ds(GR * (g % (2 * NG)), GR)]).then_inc(ids_taken, 1)
                await_(pool, ids_taken, g + 1)

            def gather_u(g, q, j):
                await_(pool, u_free, GR * g + j + 1)
                pool.indirect_dma_start(u_rows[:, j, :], None, u_tab,
                                        bass.IndirectOffsetOnAxis(ids[:, q, j:j + 1], 0)).then_inc(u_in[j], 16)

            def gather_v(g, q, j):
                await_(pool, v_free, GR * g + j + V_START - VR + 1)
                pool.indirect_dma_start(v_rows[:, j % VR, :], None, v_tab,
                                        bass.IndirectOffsetOnAxis(ids[:, q, j:j + 1], 0)).then_inc(v_in[j % VR], 16)

            u_tab = peer_u.rearrange("l e d -> (l e) d")
            v_tab = peer_v.rearrange("l e d -> (l e) d")

            def turn(g, first=False, last=False):
                for q in range(TURN):
                    nq, pq = (q + 1) % TURN, (q - 1) % TURN
                    more = not (last and q == TURN - 1)
                    if not (first and q == 0):
                        for j in range(VR, GR):
                            gather_v(g + q - 1, pq, j)
                    if more:
                        take_ids(g + q + 1, nq, fresh=first and nq > 0)
                    for j in range(GR):
                        if j < VR:
                            gather_v(g + q, q, j)
                        if more:
                            gather_u(g + q + 1, nq, j)
                if last:
                    for j in range(VR, GR):
                        gather_v(g + TURN - 1, TURN - 1, j)

            take_ids(0, 0, fresh=True)
            for j in range(GR):
                gather_u(0, 0, j)
            turn(0, first=True)
            with pool.Fori(TURN, STEPS * NG - TURN, TURN) as g:
                turn(g)
            turn(STEPS * NG - TURN, last=True)

        @block.vector
        def _(dve):
            v = nc.vector
            dve.sem_inc(ks_used, 1)

            def rsqrt(var, n, y, t):
                yi = y.bitcast(I32)
                v.tensor_scalar(yi, var.bitcast(I32), -0.5, 1597463007.0, ALU.mult, ALU.add)
                dve.drain()
                for _ in range(3):
                    v.tensor_tensor(t, y, var, ALU.mult)
                    dve.drain()
                    v.scalar_tensor_tensor(t, t, -0.5, y, ALU.mult, ALU.mult)
                    dve.drain()
                    v.scalar_tensor_tensor(y, t, 1.5, y, ALU.add, ALU.mult)
                    dve.drain()

            def row_rstd(src, sq, width):
                v.tensor_tensor_reduce(out=sq, in0=src, in1=src, scale=1.0, scalar=0.0, op0=ALU.mult,
                                       op1=ALU.add, accum_out=small[:, 0:1])
                dve.drain()
                v.tensor_scalar(small[:, 0:1], small[:, 0:1], 1.0 / width, EPS, ALU.mult, ALU.add)
                dve.drain()
                rsqrt(small[:, 0:1], 1, small[:, 1:2], small[:, 2:3])

            def head_rstd(src, sq, n, width):
                v.tensor_tensor(sq, src, src, ALU.mult)
                dve.drain()
                v.tensor_reduce(small[:, 8:8 + n], sq.rearrange("p (h d) -> p h d", h=n), AX.X, ALU.add)
                dve.drain()
                v.tensor_scalar(small[:, 8:8 + n], small[:, 8:8 + n], 1.0 / width, EPS, ALU.mult, ALU.add)
                dve.drain()
                rsqrt(small[:, 8:8 + n], n, small[:, 16:16 + n], small[:, 24:24 + n])

            def heads(ap, n):
                return ap.rearrange("p (h d) -> p h d", h=n)

            def per_head(n, width):
                return small[:, 16:16 + n][:, :, None].to_broadcast([P, n, width])

            def experts(g, i):
                for j in range(GR):
                    dve.wait_ge(u_in[j], 16 * (g + 1))
                    v.tensor_tensor_reduce(out=u_rows[:, j, :], in0=u_rows[:, j, :], in1=xn_cur[:], scale=1.0,
                                           scalar=0.0, op0=ALU.mult, op1=ALU.add,
                                           accum_out=hid[:, j:j + 1]).then_inc(u_free, 1)
                dve.drain()
                v.tensor_tensor(hid_e[:], hid[:], hid[:], ALU.mult)
                dve.drain()
                v.tensor_scalar(hid_e[:], hid_e[:], GELU_A, 1.0, ALU.mult, ALU.add)
                dve.drain()
                v.scalar_tensor_tensor(hid_e[:], hid_e[:], GELU_C, hid[:], ALU.mult, ALU.mult)
                dve.drain()
                v.tensor_scalar(hid_e[:], hid_e[:], EXP_CAP, None, ALU.min).then_inc(hid_arg, 1)
                v.tensor_tensor(hid[:], hid[:], gates_cur[:, bass.ds(GR * i, GR)], ALU.mult)
                dve.wait_ge(hid_exp, g + 1)
                v.tensor_scalar(hid_e[:], hid_e[:], 1.0, None, ALU.add)
                dve.drain()
                v.reciprocal(hid_e[:], hid_e[:])
                dve.drain()
                await_(dve, diag_ready, 2 * g + 1)
                v.tensor_tensor(hid_w[:], hid_e[:], hid[:], ALU.mult).then_inc(w_ready, 1)
                dve.drain()

            def normed(s):
                b = s % NB
                layer = s // NB
                await_(dve, x_in, 16 * (s + 1))
                v.tensor_copy(gcur[:], gains[:].rearrange("p l g -> p (l g)")[:, bass.ds(GN * layer, GN)])
                v.tensor_copy(rope_cur[:], rope_tab[:].rearrange("p b r -> p (b r)")[:, bass.ds(ROPE * b, ROPE)])
                v.tensor_scalar(state[:].rearrange("p a n -> p (a n)"), state[:].rearrange("p a n -> p (a n)"),
                                keep[:, bass.ds(b, 1)], None, ALU.mult)
                row_rstd(x_norm, part(D, D), D)
                v.tensor_scalar(x_norm, x_norm, small[:, 1:2], None, ALU.mult).then_inc(norm_ready, 1)
                await_(dve, normT, s + 1)
                v.tensor_tensor(nT[:], banks(0, 2).rearrange("p (k n) -> p k n", k=KC),
                                gcur[:, G_MIX:G_MIX + KC][:, :, None].to_broadcast([P, KC, P]),
                                ALU.mult).then_inc(nT_ready, 1)

            def front(s, body, last=False):
                first = isinstance(s, int) and s == 0
                b = s % NB
                layer = s // NB
                body(0)
                await_(dve, uv_out, s + 1)
                uv = uvc[:, 0:2 * GM_W]
                v.tensor_tensor(gl, uv, uv, ALU.mult)
                dve.drain()
                v.tensor_scalar(gl, gl, GELU_A, 1.0, ALU.mult, ALU.add)
                dve.drain()
                v.scalar_tensor_tensor(gl, gl, GELU_C, uv, ALU.mult, ALU.mult)
                dve.drain()
                v.tensor_scalar(gl, gl, EXP_CAP, None, ALU.min).then_inc(gelu_arg, 1)
                cq = uvc[:, 2 * GM_W:2 * GM_W + QR]
                ckv = uvc[:, 2 * GM_W + QR:2 * GM_W + QR + KVR]
                row_rstd(cq, cn[:, 0:QR], QR)
                v.tensor_scalar(cn[:, 0:QR], cq, small[:, 1:2], None, ALU.mult)
                dve.drain()
                row_rstd(ckv, cn[:, QR:QR + KVR], KVR)
                v.tensor_scalar(cn[:, QR:QR + KVR], ckv, small[:, 1:2], None, ALU.mult).then_inc(lat_ready, 1)
                body(1)
                if not first:
                    await_(dve, x_stored, 16 * s)
                await_(dve, chunk_free, used(s, CH_GM))
                v.tensor_tensor(heads(gmT, GM_HEADS), heads(banks(0, 1), GM_HEADS),
                                tri[:, None, :].to_broadcast([P, GM_HEADS, P]), ALU.mult).then_inc(gmT_ready, 1)
                await_(dve, gelu_exp, s + 1)
                v.tensor_scalar(gl, gl, 1.0, None, ALU.add)
                dve.drain()
                v.reciprocal(gl, gl)
                dve.drain()
                v.tensor_tensor(uv, uv, gl, ALU.mult)
                dve.drain()
                vv = uvc[:, GM_W:2 * GM_W]
                head_rstd(vv, gl[:, 0:GM_W], GM_HEADS, GM_DIM)
                v.tensor_tensor(heads(vv, GM_HEADS), heads(vv, GM_HEADS), per_head(GM_HEADS, GM_DIM),
                                ALU.mult).then_inc(vhat, 1)
                await_(dve, latT, s + 1)
                v.tensor_tensor(heads(cT, 3), heads(banks(2, 1)[:, 0:384], 3),
                                gcur[:, G_Q:G_Q + 3][:, :, None].to_broadcast([P, 3, P]),
                                ALU.mult).then_inc(latT_ready, 1)
                body(2)
                await_(dve, z_ps, s + 1)
                await_(dve, gvn_in, 16 * (s + 1))
                z = gl[:, 0:GM_W]
                v.tensor_tensor(z, banks(1, 1)[:, 0:GM_W], gvn[:], ALU.mult)
                dve.drain()
                v.tensor_tensor(heads(z, GM_HEADS), heads(z, GM_HEADS),
                                gcur[:, G_B:G_B + GM_HEADS][:, :, None].to_broadcast([P, GM_HEADS, GM_DIM]), ALU.add)
                dve.drain()
                v.tensor_tensor(z, z, uvc[:, 0:GM_W], ALU.mult)
                dve.drain()
                head_rstd(z, gl[:, GM_W:2 * GM_W], GM_HEADS, GM_DIM)
                v.tensor_tensor(heads(feat[:, 0:GM_W], GM_HEADS), heads(z, GM_HEADS), per_head(GM_HEADS, GM_DIM),
                                ALU.mult)
                body(3)
                await_(dve, qkv_out, s + 1)
                q3 = heads(qs, AH)
                cosq = rope_cur[:, None, 0:HALF].to_broadcast([P, AH, HALF])
                sinq = rope_cur[:, None, HALF:ROPE].to_broadcast([P, AH, HALF])
                t = [heads(rt[:, i * P:(i + 1) * P], AH) for i in range(4)]
                q1, q2 = q3[:, :, NOPE:NOPE + HALF], q3[:, :, NOPE + HALF:QK]
                v.tensor_tensor(t[0], q1, cosq, ALU.mult)
                v.tensor_tensor(t[1], q2, sinq, ALU.mult)
                v.tensor_tensor(t[2], q2, cosq, ALU.mult)
                v.tensor_tensor(t[3], q1, sinq, ALU.mult)
                k1 = uvc[:, TOKW - ROPE:TOKW - HALF]
                k2 = uvc[:, TOKW - HALF:TOKW]
                kt = [kr[:, i * HALF:(i + 1) * HALF] for i in range(6)]
                v.tensor_tensor(kt[0], k1, rope_cur[:, 0:HALF], ALU.mult)
                v.tensor_tensor(kt[1], k2, rope_cur[:, HALF:ROPE], ALU.mult)
                v.tensor_tensor(kt[2], k2, rope_cur[:, 0:HALF], ALU.mult)
                v.tensor_tensor(kt[3], k1, rope_cur[:, HALF:ROPE], ALU.mult)
                dve.drain()
                v.tensor_tensor(q3[:, :, NOPE:NOPE + HALF], t[0], t[1], ALU.subtract)
                v.tensor_tensor(q3[:, :, NOPE + HALF:QK], t[2], t[3], ALU.add)
                v.tensor_tensor(kt[4], kt[0], kt[1], ALU.subtract)
                v.tensor_tensor(kt[5], kt[2], kt[3], ALU.add)
                dve.drain()
                v.tensor_copy(heads(kf, AH)[:, :, NOPE:QK],
                              kr[:, None, 4 * HALF:6 * HALF].to_broadcast([P, AH, ROPE])).then_inc(roped, 1)
                await_(dve, proj_out, s + 1)
                qf2 = qf[:].rearrange("p a n -> p (a n)")
                v.tensor_scalar(e4[:, 0:2 * HG_W], qf2, -1.0, EXP_CAP, ALU.mult, ALU.min)
                v.tensor_scalar(e4[:, 2 * HG_W:3 * HG_W], qf2[:, HG_W:2 * HG_W], EXP_CAP, None, ALU.min)
                v.tensor_scalar(e4[:, 3 * HG_W:4 * HG_W], ig[:, HG_W:2 * HG_W], -1.0, EXP_CAP, ALU.mult,
                                ALU.min).then_inc(hg_arg, 1)
                body(4)
                await_(dve, qkT_ps, s + 1)
                v.memset(aT, 0.0)
                await_(dve, hg_exp, s + 1)
                v.tensor_scalar(e4, e4, 1.0, None, ALU.add)
                dve.drain()
                v.reciprocal(e4, e4)
                dve.drain()
                v.tensor_tensor(hq, qf2[:, 0:HG_W], e4[:, 0:HG_W], ALU.mult)
                for a in range(HP):
                    at = slice(a * P, (a + 1) * P)
                    v.tensor_scalar(hk[:, at], e4[:, 2 * HG_W:3 * HG_W][:, at], gcur[:, G_OM + a:G_OM + a + 1], None,
                                    ALU.mult)
                    v.tensor_scalar(e4[:, HG_W:2 * HG_W][:, at], e4[:, HG_W:2 * HG_W][:, at],
                                    gcur[:, G_OM + a:G_OM + a + 1], gcur[:, G_LB + a:G_LB + a + 1], ALU.mult, ALU.add)
                v.tensor_tensor(ig[:, HG_W:2 * HG_W], ig[:, HG_W:2 * HG_W], e4[:, 3 * HG_W:4 * HG_W], ALU.mult)
                dve.drain()
                lf = e4[:, HG_W:2 * HG_W]
                v.tensor_scalar(lf, lf, GATE_FLOOR, None, ALU.max).then_inc(f_ready, 1)
                await_(dve, lnf, s + 1)
                v.tensor_scalar(lf, lf, -math.log(LN_SHIFT), None, ALU.add)
                dve.drain()
                cum = wl[:, 8 * HG_W:9 * HG_W]
                for a in range(HP):
                    v.tensor_tensor_scan(cum[:, a * P:(a + 1) * P], ones[:], lf[:, a * P:(a + 1) * P], 0.0,
                                         ALU.mult, ALU.add)
                dve.drain()
                for m, h in enumerate(LEVELS):
                    c4 = cum.rearrange("p (g r) -> p g r", r=2 * h)
                    v.tensor_tensor(wl[:, m * HG_W:(m + 1) * HG_W].rearrange("p (g r) -> p g r", r=2 * h), c4,
                                    c4[:, :, h - 1:h].to_broadcast([P, HG_W // (2 * h), 2 * h]), ALU.subtract)
                c3 = heads(cum, HP)
                v.tensor_tensor(heads(wl[:, 7 * HG_W:8 * HG_W], HP), c3, c3[:, :, P - 1:P].to_broadcast([P, HP, P]),
                                ALU.subtract).then_inc(dist, 1)
                body(5)
                await_(dve, decay, s + 1)
                v.tensor_tensor(kd, hk, wl[:, 7 * HG_W:8 * HG_W], ALU.mult).then_inc(kd_ready, 1)

                def keep_level(m):
                    await_(dve, level_ps, (NL + 1) * s + m + 1)
                    e = m % 2
                    v.copy_predicated(aT.rearrange("p (x a n) -> p x a n", x=2, a=HP),
                                      pair_mask[:, m, :][:, None, None, :].to_broadcast([P, 2, HP, P]),
                                      bank[:, 2 + 2 * e:4 + 2 * e, 0:HP * P].rearrange("p x (a n) -> p x a n", a=HP)
                                      ).then_inc(level_used, 1)
                    dve.drain()

                for m in range(NL):
                    e = m % 2
                    w = wl[:, m * HG_W:(m + 1) * HG_W]
                    if m >= 2:
                        keep_level(m - 2)
                    v.tensor_tensor(q_l[:, e * HG_W:(e + 1) * HG_W], hq, w, ALU.mult)
                    v.tensor_tensor(k_l[:, e * HG_W:(e + 1) * HG_W], hk, w, ALU.mult).then_inc(level_ready, 1)
                for m in (NL - 2, NL - 1, NL):
                    keep_level(m)
                v.tensor_tensor(q_l[:, 0:HG_W], hq, wl[:, 8 * HG_W:9 * HG_W], ALU.mult).then_inc(c_done, 1)
                body(6)
                await_(dve, o_ps, s + 1)
                for a in range(HP):
                    for e in range(2):
                        r = slice(64 * e, 64 * e + 64)
                        v.scalar_tensor_tensor(state[r, a, r], state[r, a, r],
                                               wl[r, 8 * HG_W + a * P + P - 1:8 * HG_W + a * P + P],
                                               bank[r, 0, HG_W + a * P + 64 * e:HG_W + a * P + 64 * e + 64],
                                               ALU.mult, ALU.add)
                v.tensor_copy(o_sb, banks(0, 1)[:, 0:HG_W])
                dve.drain()
                head_rstd(o_sb, o_sq, 4, 64)
                v.tensor_tensor(heads(o_sb, 4), heads(o_sb, 4), per_head(4, 64), ALU.mult)
                dve.drain()
                v.tensor_tensor(feat[:, 768:1024], o_sb, ig[:, HG_W:2 * HG_W], ALU.mult)
                dve.drain()

                def attend(hp, i=None):
                    for e in range(2):
                        n = AH * s + 2 * hp + e + 1
                        se = sc[:, e * SEQ:(e + 1) * SEQ]
                        await_(dve, s_ps, n)
                        v.scalar_tensor_tensor(se, banks(2 + e, 1), ATT_SCALE, causal[:, bass.ds(P * (3 - b), SEQ)],
                                               ALU.mult, ALU.add)
                        dve.drain()
                        v.tensor_reduce(small[:, 34 + e:35 + e], se, AX.X, ALU.max)
                        dve.drain()
                        v.tensor_scalar(small[:, 36 + e:37 + e], small[:, 34 + e:35 + e], -1.0, None,
                                        ALU.mult).then_inc(s_max, 1)
                    if i is not None:
                        body(i)
                    for e in range(2):
                        n = AH * s + 2 * hp + e + 1
                        await_(dve, att_ps, n)
                        v.reciprocal(small[:, 40 + e:41 + e], small[:, 38 + e:39 + e])
                        dve.drain()
                        v.tensor_scalar(feat[:, bass.ds(256 + 2 * VD * hp + VD * e, VD)], bank[:, e, 0:VD],
                                        small[:, 40 + e:41 + e], None, ALU.mult).then_inc(att_out, 1)
                    dve.drain()

                with dve.Fori(0, AH // 4) as q:
                    attend(2 * q, q + 7)
                    attend(2 * q + 1)
                head_rstd(feat[:, 256:768], y_sq, AH, VD)
                v.tensor_tensor(heads(feat[:, 256:768], AH), heads(feat[:, 256:768], AH), per_head(AH, VD),
                                ALU.mult).then_inc(y_ready, 1)
                await_(dve, yT_ps, s + 1)
                v.tensor_tensor(nT[:], banks(0, 2).rearrange("p (k n) -> p k n", k=KC),
                                gcur[:, G_Y:G_Y + KC][:, :, None].to_broadcast([P, KC, P]),
                                ALU.mult).then_inc(yT_ready, 1)
                body(9)
                await_(dve, chunk_free, used(s, CH_WO + KC - 1))
                await_(dve, res_in, 16 * (s + 1))
                v.tensor_tensor(x_cur[:], x_cur[:], banks(2, 2), ALU.add)
                dve.drain()
                row_rstd(x_cur[:], x_sq, D)
                v.tensor_scalar(feat[:], x_cur[:], small[:, 1:2], None, ALU.mult)
                dve.drain()
                await_(dve, gain_in, 16 * (s + 1))
                v.tensor_tensor(feat[:], feat[:], qT[:], ALU.mult).then_inc(xn_ready, 1)
                body(10)

                def sixteen(jobs):
                    for r in range(2):
                        eight = slice(8 * r, 8 * r + 8)
                        for src, spare, dst, index in jobs:
                            v.max(dst[:, eight], spare if r else src)
                        dve.drain()
                        for src, spare, dst, index in jobs:
                            v.max_index(index[:, eight], dst[:, eight], spare if r else src)
                            if r == 0:
                                v.match_replace(spare, dst[:, eight], src, -3e38)
                        dve.drain()

                def of(ap, i, n):
                    return ap[:, i * n:(i + 1) * n]

                def route(hp):
                    body(hp + 11)
                    await_(dve, ks_ready, PH * s + 2 * hp + 2)
                    sixteen([(of(ks, i, NK), of(ks2, i, NK), of(top, i, TK), of(topu, i, TK)) for i in range(4)])
                    v.tensor_copy(topi, topu)
                    for e in range(2):
                        ins = v.tensor_tensor(of(cand, e, TK * TK).rearrange("p (i j) -> p i j", i=TK),
                                              of(top, 2 * e, TK)[:, :, None].to_broadcast([P, TK, TK]),
                                              of(top, 2 * e + 1, TK)[:, None, :].to_broadcast([P, TK, TK]), ALU.add)
                    ins.then_inc(ks_used, 2)
                    dve.drain()
                    sixteen([(of(cand, e, TK * TK), of(hot, e, TK * TK), of(picked, e, TK), of(posu, e, TK))
                             for e in range(2)])
                    h3 = halfu.rearrange("p (e c k) -> p e c k", e=2, c=2)
                    p3 = posu.rearrange("p (e k) -> p e k", e=2)
                    v.tensor_scalar(h3[:, :, 0, :], p3, 4, None, ALU.logical_shift_right)
                    v.tensor_scalar(h3[:, :, 1, :], p3, 15, None, ALU.bitwise_and)
                    v.tensor_copy(best[:, bass.ds(2 * TK * hp, 2 * TK)], picked)
                    dve.drain()
                    v.tensor_copy(halff, halfu)
                    dve.drain()
                    one_hot = hot.rearrange("p (x k j) -> p x k j", x=4, k=TK)
                    v.tensor_tensor(hot.rearrange("p (k j) -> p k j", j=TK), halff[:, :, None].to_broadcast([P, 4 * TK, TK]),
                                    iota16[:, None, :].to_broadcast([P, 4 * TK, TK]), ALU.is_equal)
                    dve.drain()
                    for i in range(4):
                        v.tensor_tensor(one_hot[:, i], one_hot[:, i],
                                        of(topi, i, TK)[:, None, :].to_broadcast([P, TK, TK]), ALU.mult)
                    dve.drain()
                    v.tensor_reduce(chosen, hot.rearrange("p (k j) -> p k j", j=TK), AX.X, ALU.add)
                    dve.drain()
                    c3 = chosen.rearrange("p (e c k) -> p e c k", e=2, c=2)
                    v.scalar_tensor_tensor(idf[:, bass.ds(2 * TK * hp, 2 * TK)].rearrange("p (e k) -> p e k", e=2),
                                           c3[:, :, 0, :], float(NK), c3[:, :, 1, :], ALU.mult, ALU.add)
                    dve.drain()

                with dve.Fori(0, PH // 2) as hp:
                    route(hp)
                v.tensor_scalar(idf, idf, layer_base[:, bass.ds(layer, 1)], None, ALU.add)
                b3 = heads(best, PH)
                g3 = heads(gates_next[:], PH)
                v.tensor_tensor(g3, b3, b3[:, :, 0:1].to_broadcast([P, PH, TK]), ALU.subtract).then_inc(sm_arg, 1)
                dve.drain()
                v.tensor_copy(ids_ring[:, bass.ds(SLOTS * (s % 2), SLOTS)], idf).then_inc(ids_ready, 1)
                await_(dve, sm_exp, s + 1)
                v.tensor_reduce(gsum[:, 0:PH], g3, AX.X, ALU.add)
                dve.drain()
                v.reciprocal(gsum[:, PH:2 * PH], gsum[:, 0:PH])
                dve.drain()
                v.tensor_tensor(g3, g3, gsum[:, PH:2 * PH][:, :, None].to_broadcast([P, PH, TK]), ALU.mult)
                body(15)
                dve.drain()
                v.tensor_copy(xn_cur[:], feat[:])
                v.tensor_copy(gates_cur[:], gates_next[:])
                if not last:
                    normed(s + 1)
                if not first:
                    await_(dve, v_free, V_START + SLOTS * s)
                    v.tensor_copy(x_rows, vsum[:]).then_inc(x_new, 1)
                dve.drain()

            layer_base = small[:, 60:62]
            v.memset(small[:], 0.0)
            inv_freq = part(SETUP + 256, HALF)
            freqs = np.exp(np.float32(-math.log(10000.0)) * np.arange(HALF, dtype=np.float32) / np.float32(HALF))
            dve.drain()
            v.memset(small[:, 61:62], float(NK * NK))
            for i in range(HALF):
                v.memset(inv_freq[:, i:i + 1], float(np.float32(freqs[i])))
            posf32 = part(SETUP + 272, NB)
            dve.wait_ge(pos_in, 16)
            v.tensor_copy(posf32, pos_i[:])
            dve.drain()
            ang, turns, red = (part(SETUP + 288 + i * NB * HALF, NB * HALF) for i in range(3))
            v.tensor_tensor(heads(ang, NB), posf32[:, :, None].to_broadcast([P, NB, HALF]),
                            inv_freq[:, None, :].to_broadcast([P, NB, HALF]), ALU.mult)
            dve.drain()
            two_pi = 2.0 * math.pi
            hi = 6.28125
            mid = float(np.float32(np.round((two_pi - hi) * 2.0 ** 20) / 2.0 ** 20))
            lo = two_pi - hi - mid
            magic = 1.5 * 2.0 ** 23
            for quarter, col in ((0.25, 0), (0.0, HALF)):
                v.tensor_scalar(turns, ang, 1.0 / two_pi, quarter, ALU.mult, ALU.add)
                dve.drain()
                v.tensor_scalar(turns, turns, magic, None, ALU.add)
                dve.drain()
                v.tensor_scalar(turns, turns, -magic, None, ALU.add)
                dve.drain()
                v.scalar_tensor_tensor(red, turns, -hi, ang, ALU.mult, ALU.add)
                dve.drain()
                v.scalar_tensor_tensor(red, turns, -mid, red, ALU.mult, ALU.add)
                dve.drain()
                v.scalar_tensor_tensor(red, turns, -lo, red, ALU.mult, ALU.add)
                dve.drain()
                v.tensor_scalar(red, red, quarter * two_pi, 3.1415925, ALU.add, ALU.min)
                dve.drain()
                v.tensor_scalar(rope_tab[:, :, col:col + HALF], heads(red, NB), -3.1415925, None,
                                ALU.max).then_inc(rope_arg, 1)
                dve.drain()
            dve.wait_ge(rowsT, 1)
            v.tensor_copy(gains[:, :, 0:ROWS], bank[:, 0, 0:DEPTH * ROWS].rearrange("p (l g) -> p l g", l=DEPTH)
                          ).then_inc(gains_ready, 1)
            dve.drain()
            l0, l1 = gains[:, 0, G_LB:G_LB + 2], gains[:, 1, G_LB:G_LB + 2]
            mx, e0, e1, tot = small[:, 44:46], small[:, 46:48], small[:, 48:50], small[:, 50:52]
            v.tensor_tensor(mx, l0, l1, ALU.max)
            dve.drain()
            v.tensor_tensor(e0, l0, mx, ALU.subtract)
            v.tensor_tensor(e1, l1, mx, ALU.subtract).then_inc(lb_arg, 1)
            dve.wait_ge(lb_exp, 1)
            v.tensor_tensor(tot, e0, e1, ALU.add)
            dve.drain()
            v.reciprocal(tot, tot)
            dve.drain()
            v.tensor_tensor(e0, e0, tot, ALU.mult)
            v.tensor_tensor(e1, e1, tot, ALU.mult)
            dve.drain()
            v.tensor_tensor(l0, e0, e0, ALU.subtract)
            v.tensor_tensor(tot, e0, e1, ALU.add)
            dve.drain()
            v.tensor_tensor(l1, tot, e0, ALU.subtract)
            dve.drain()
            v.tensor_scalar(gains[:, :, G_OM:G_OM + 2], gains[:, :, G_LB:G_LB + 2], -1.0, 1.0, ALU.mult, ALU.add)
            dve.drain()
            dve.wait_ge(consts, 3)
            dve.wait_ge(tables_ready, 1)
            normed(0)
            front(0, lambda i: None)
            with dve.Fori(1, STEPS - 1) as s:
                front(s, lambda i: experts((s - 1) * NG + i, i))
            front(STEPS - 1, lambda i: experts((STEPS - 2) * NG + i, i), last=True)

            def final(b):
                row_rstd(x_cur[:], scr[:, 0:D], D)
                if b:
                    dve.wait_ge(fin_out, 16 * b)
                v.tensor_scalar(feat[:], x_cur[:], small[:, 1:2], None, ALU.mult)
                dve.drain()
                v.tensor_tensor(feat[:], feat[:], qT[:], ALU.mult).then_inc(fin_ready, 1)

            last = (STEPS - 1) * NG
            experts(last, 0)
            dve.wait_ge(gainf_in, 16)
            for b in range(NB - 1):
                dve.wait_ge(fin_in, 16 * (b + 1))
                final(b)
                experts(last + b + 1, b + 1)
            with dve.Fori(NB, NG) as i:
                experts(last + i, i)
            dve.wait_ge(v_free, V_START + SLOTS * STEPS)
            v.tensor_copy(x_cur[:], vsum[:])
            dve.drain()
            final(NB - 1)

        @block.scalar
        def _(act):
            a_ = nc.scalar
            act.sem_inc(diag_ready, 1)

            def experts(g, i):
                act.wait_ge(hid_arg, g + 1)
                a_.activation(hid_e[:], hid_e[:], ACT.Exp).then_inc(hid_exp, 1)
                act.wait_ge(w_ready, g + 1)
                for half in range(2):
                    await_(act, v_free, GR * (g - 1) + VR * (half + 1) + V_START)
                    for j in range(VR * half, VR * half + VR):
                        ins = a_.activation(diag[:, j, :], ident[:], ACT.Copy, scale=hid_w[:, j:j + 1])
                    ins.then_inc(diag_ready, 1)

            def front(s, body):
                b = s % NB
                body(0)
                await_(act, proj_uv, s + 1)
                a_.activation(uvc, banks(2, 2)[:, 0:TOKW], ACT.Copy).then_inc(uv_out, 1)
                await_(act, gelu_arg, s + 1)
                a_.activation(gl, gl, ACT.Exp).then_inc(gelu_exp, 1)
                body(1)
                await_(act, proj, s + 1)
                a_.activation(ig[:], banks(4, 1), ACT.Copy)
                a_.activation(qf[:].rearrange("p a n -> p (a n)"), banks(5, 1), ACT.Copy).then_inc(proj_out, 1)
                await_(act, chunk_free, used(s, CH_UKV))
                a_.activation(qs, banks(4, 2)[:, 0:AH * QK], ACT.Copy)
                kv = banks(2, 2).rearrange("p (h d) -> p h d", h=AH)
                a_.activation(kf.rearrange("p (h d) -> p h d", h=AH)[:, :, 0:NOPE], kv[:, :, 0:NOPE], ACT.Copy)
                a_.activation(v_cache[:].rearrange("p b n -> p (b n)")[:, bass.ds(AH * VD * b, AH * VD)].rearrange(
                    "p (h d) -> p h d", h=AH), kv[:, :, NOPE:NOPE + VD], ACT.Copy).then_inc(qkv_out, 1)
                body(2)
                body(3)
                await_(act, hg_arg, s + 1)
                a_.activation(e4, e4, ACT.Exp).then_inc(hg_exp, 1)
                body(4)
                await_(act, f_ready, s + 1)
                lf = e4[:, HG_W:2 * HG_W]
                a_.activation(lf, lf, ACT.Ln, scale=LN_SHIFT).then_inc(lnf, 1)
                await_(act, qkT_ps, s + 1)
                a_.activation(qT[0:QK, :], banks(0, 2)[0:QK, :], ACT.Copy)
                a_.activation(k_cache[:, :, bass.ds(P * b, P)],
                              banks(4, 2)[0:QK, :].rearrange("p (h n) -> p h n", h=AH), ACT.Copy).then_inc(qkT_ready, 1)
                await_(act, dist, s + 1)
                a_.activation(wl, wl, ACT.Abs)
                act.drain()
                a_.activation(wl, wl, ACT.Exp, scale=-1.0).then_inc(decay, 1)
                body(5)
                await_(act, kdT_ps, s + 1)
                a_.activation(kdT, banks(1, 1)[:, 0:HG_W], ACT.Copy).then_inc(kdT_ready, 1)
                body(6)

                def attend(hp, i=None):
                    for e in range(2):
                        se = sc[:, e * SEQ:(e + 1) * SEQ]
                        await_(act, s_max, AH * s + 2 * hp + e + 1)
                        a_.activation(se, se, ACT.Exp, bias=small[:, 36 + e:37 + e],
                                      accum_out=small[:, 38 + e:39 + e]).then_inc(p_ready, 1)
                    for e in range(2):
                        await_(act, pT_ps, AH * s + 2 * hp + e + 1)
                        a_.activation(pT[:, e * SEQ:(e + 1) * SEQ], banks(4 + e, 1), ACT.Copy).then_inc(pT_ready, 1)
                    if i is not None:
                        body(i)

                with act.Fori(0, AH // 4) as q:
                    attend(2 * q, q + 7)
                    attend(2 * q + 1)
                body(9)
                await_(act, xnT_ps, s + 1)
                a_.activation(nT[:].rearrange("p k n -> p (k n)"), banks(0, 2), ACT.Copy).then_inc(xnT_ready, 1)
                body(10)
                await_(act, chunk_free, used(s, CH_WQ + PH - 1))
                a_.activation(qpT, banks(4, 2), ACT.Copy).then_inc(qp_ready, 1)
                await_(act, chunk_free, used(s, CH_SK))
                a_.activation(subT, banks(2, 2), ACT.Copy).then_inc(skT_ready, 1)

                await_(act, keys_ps, s + 1)

                def hand_scores(hp):
                    for e in range(2):
                        await_(act, ks_used, PH * s + 2 * hp + 1)
                        a_.activation(ks[:, e * 2 * NK:(e + 1) * 2 * NK].rearrange("p (c n) -> p c n", c=2),
                                      banks(0, 4).rearrange("p (c n) -> p c n", c=2)[:, :, bass.ds(NK * (2 * hp + e), NK)],
                                      ACT.Copy).then_inc(ks_ready, 1)

                hand_scores(0)
                body(11)
                with act.Fori(1, PH // 2) as hp:
                    hand_scores(hp)
                    body(hp + 11)
                await_(act, sm_arg, s + 1)
                a_.activation(gates_next[:], gates_next[:], ACT.Exp).then_inc(sm_exp, 1)
                body(15)

            act.wait_ge(rope_arg, 2)
            rt_all = rope_tab[:].rearrange("p b r -> p (b r)")
            a_.activation(rt_all, rt_all, ACT.Sin).then_inc(tables_ready, 1)
            act.wait_ge(lb_arg, 1)
            a_.activation(small[:, 46:50], small[:, 46:50], ACT.Exp).then_inc(lb_exp, 1)
            act.wait_ge(consts, 3)
            front(0, lambda i: None)
            with act.Fori(1, STEPS - 1) as s:
                front(s, lambda i: experts((s - 1) * NG + i, i))
            front(STEPS - 1, lambda i: experts((STEPS - 2) * NG + i, i))
            last = (STEPS - 1) * NG
            with act.Fori(0, NG) as i:
                experts(last + i, i)

        @block.tensor
        def _(pe):
            mm = nc.tensor.matmul

            def transposes(dst, src, n, width):
                for k in range(n):
                    last = nc.tensor.transpose(dst[0:width, k * P:(k + 1) * P], src[:, k * width:(k + 1) * width], ident[:])
                return last

            def chunk(s, c):
                pe.wait_ge(chunk_in[c % RING], 16 * (NCH // RING * s + c // RING + 1))
                return ring[:, c % RING, :]

            def experts(g, half):
                pe.wait_ge(diag_ready, 2 * g + half + 2)
                for j in range(VR * half, VR * half + VR):
                    pe.wait_ge(v_in[j % VR], 16 * (2 * g + half + 1))
                    for n in range(2):
                        ins = mm(vsum[:, n * 512:(n + 1) * 512], diag[:, j, :], v_rows[:, j % VR, n * 512:(n + 1) * 512],
                                 start=False, stop=False, skip_group_check=True)
                    ins.then_inc(v_free, 1)

            def normed(s):
                pe.wait_ge(norm_ready, s + 1)
                transposes(banks(0, 2), x_norm, KC, P).then_inc(normT, 1)

            def front(s, body, last_step=False):
                first = isinstance(s, int) and s == 0
                layer = s // NB
                pe.wait_ge(nT_ready, s + 1)
                pe.wait_ge(win_in, 16 * (layer + 1))

                def tokens(dst, c0, n):
                    for k in range(KC):
                        last = mm(dst[:, 0:n], nT[:, k, :], win[:, k, c0:c0 + n], start=k == 0, stop=k == KC - 1)
                    return last

                tokens(banks(2, 1), 0, 512)
                tokens(banks(3, 1), 512, TOKW - 512).then_inc(proj_uv, 1)
                transposes(banks(0, 1), chunk(s, CH_GM), GM_HEADS, P).then_inc(chunk_free, 1)
                body(0, 0)
                tokens(banks(4, 1), C_HI, 512)
                pe.wait_ge(lat_ready, s + 1)
                pe.wait_ge(uv_out, s + 1)
                transposes(banks(2, 1), cn, 3, P).then_inc(latT, 1)
                body(0, 1)
                for a in range(4):
                    for k in range(KC):
                        last = mm(banks(5, 1)[:, a * P:(a + 1) * P], win[:, k, C_HQ + a * P:C_HQ + (a + 1) * P],
                                  nT[:, k, :], start=k == 0, stop=k == KC - 1)
                last.then_inc(proj, 1)
                body(1, 0)
                pe.wait_ge(gmT_ready, s + 1)
                pe.wait_ge(vhat, s + 1)
                for h in range(GM_HEADS):
                    last = mm(banks(1, 1)[:, h * GM_DIM:(h + 1) * GM_DIM], gmT[:, h * P:(h + 1) * P],
                              uvc[:, GM_W + h * GM_DIM:GM_W + (h + 1) * GM_DIM], start=True, stop=True)
                last.then_inc(z_ps, 1)
                pe.wait_ge(latT_ready, s + 1)
                pe.wait_ge(proj_out, s + 1)
                for k in range(2):
                    w = chunk(s, CH_UQ + k)
                    for c0, n in ((0, 512), (512, 256)):
                        last = mm(banks(4, 2)[:, c0:c0 + n], cT[:, k * P:(k + 1) * P], w[:, c0:c0 + n],
                                  start=k == 0, stop=k == 1)
                    last.then_inc(chunk_free, 1)
                w = chunk(s, CH_UKV)
                for n in range(2):
                    last = mm(banks(2 + n, 1), cT[:, 2 * P:3 * P], w[:, n * 512:(n + 1) * 512], start=True, stop=True)
                last.then_inc(chunk_free, 1)
                body(1, 1)
                body(2, 0)
                body(2, 1)
                pe.wait_ge(qkv_out, s + 1)
                pe.wait_ge(roped, s + 1)
                transposes(banks(0, 2), qs, AH, QK)
                transposes(banks(4, 2), kf, AH, QK).then_inc(qkT_ps, 1)
                body(3, 0)
                body(3, 1)
                body(4, 0)
                body(4, 1)
                pe.wait_ge(kd_ready, s + 1)
                pe.wait_ge(qkT_ready, s + 1)
                transposes(banks(1, 1), kd, HP, P).then_inc(kdT_ps, 1)
                for m in range(NL + 1):
                    e = m % 2
                    if m < NL:
                        pe.wait_ge(level_ready, NL * s + m + 1)
                    if m >= 2:
                        pe.wait_ge(level_used, (NL + 1) * s + m - 1)
                    qq, kk = (q_l[:, e * HG_W:(e + 1) * HG_W], k_l[:, e * HG_W:(e + 1) * HG_W]) if m < NL else (hq, hk)
                    for h in range(4):
                        r = slice(64 * (h % 2), 64 * (h % 2) + 64)
                        c = slice(P * (h // 2), P * (h // 2) + P)
                        last = mm(bank[:, 2 + 2 * e + h % 2, c], kk[r, c], qq[r, c], start=True, stop=True)
                    last.then_inc(level_ps, 1)
                    if m == NL - 2:
                        body(5, 0)
                pe.wait_ge(c_done, s + 1)
                pe.wait_ge(kdT_ready, s + 1)
                for a in range(HP):
                    o = banks(0, 1)[:, a * P:(a + 1) * P]
                    mm(o, q_l[:, a * P:(a + 1) * P], state[:, a, :], start=True, stop=False, skip_group_check=True)
                    for e in range(2):
                        mm(o[:, 64 * e:64 * e + 64], aT[:, (2 * e + a) * P:(2 * e + a + 1) * P],
                           ig[:, (2 * a + e) * 64:(2 * a + e + 1) * 64], start=False, stop=True, skip_group_check=True)
                for a in range(HP):
                    last = mm(banks(0, 1)[:, HG_W + a * P:HG_W + (a + 1) * P], kdT[:, a * P:(a + 1) * P],
                              ig[:, a * P:(a + 1) * P], start=True, stop=True)
                last.then_inc(o_ps, 1)

                def scores(hp):
                    if hp or not first:
                        pe.wait_ge(s_max, AH * s + 2 * hp)
                    for e in range(2):
                        h = 2 * hp + e
                        mm(banks(2 + e, 1), qT[0:QK, P * h:P * (h + 1)], k_cache[:, h, :],
                           start=True, stop=True).then_inc(s_ps, 1)

                def attend(hp):
                    for e in range(2):
                        pe.wait_ge(p_ready, AH * s + 2 * hp + e + 1)
                        transposes(banks(4 + e, 1), sc[:, e * SEQ:(e + 1) * SEQ], NB, P).then_inc(pT_ps, 1)
                    if hp or not first:
                        pe.wait_ge(att_out, AH * s + 2 * hp)
                    for e in range(2):
                        h = 2 * hp + e
                        pe.wait_ge(pT_ready, AH * s + 2 * hp + e + 1)
                        for kb in range(NB):
                            last = mm(bank[:, e, 0:VD], pT[:, e * SEQ + kb * P:e * SEQ + (kb + 1) * P],
                                      v_cache[:, kb, VD * h:VD * (h + 1)], start=kb == 0, stop=kb == NB - 1)
                        last.then_inc(att_ps, 1)

                scores(0)
                body(5, 1)
                for hp in range(AH // 2):
                    body(6 + hp // 2, hp % 2)
                    attend(hp)
                    if hp + 1 < AH // 2:
                        scores(hp + 1)
                body(8, 0)
                pe.wait_ge(y_ready, s + 1)
                transposes(banks(0, 2), feat[:], KC, P).then_inc(yT_ps, 1)
                pe.wait_ge(yT_ready, s + 1)
                for k in range(KC):
                    if k == RING:
                        body(8, 1)
                    if k == 2 * RING:
                        body(9, 0)
                    w = chunk(s, CH_WO + k)
                    for n in range(2):
                        last = mm(banks(2 + n, 1), nT[:, k, :], w[:, n * 512:(n + 1) * 512], start=k == 0,
                                  stop=k == KC - 1, skip_group_check=True)
                    last.then_inc(chunk_free, 1)
                body(9, 1)
                pe.wait_ge(xn_ready, s + 1)
                transposes(banks(0, 2), feat[:], KC, P).then_inc(xnT_ps, 1)
                pe.wait_ge(xnT_ready, s + 1)
                for h in range(PH):
                    if h == 2 * RING:
                        body(10, 0)
                    w = chunk(s, CH_WQ + h)
                    for k in range(KC):
                        last = mm(banks(4, 2)[:, h * P:(h + 1) * P], w[:, k * P:(k + 1) * P], nT[:, k, :],
                                  start=k == 0, stop=k == KC - 1)
                    last.then_inc(chunk_free, 1)
                w = chunk(s, CH_SK)
                transposes(banks(2, 2), w, PH, P).then_inc(chunk_free, 1)
                pe.wait_ge(qp_ready, s + 1)
                pe.wait_ge(skT_ready, s + 1)
                for h in range(PH):
                    for c in range(2):
                        r = slice(64 * c, 64 * c + 64)
                        last = mm(banks(2 * c, 2)[:, h * NK:(h + 1) * NK], qpT[r, h * P:(h + 1) * P],
                                  subT[r, h * P:(h + 1) * P], start=True, stop=True)
                last.then_inc(keys_ps, 1)
                body(10, 1)
                with pe.Fori(11, NG - 1) as i:
                    body(i, 0)
                    body(i, 1)
                body(NG - 1, 0)
                if not last_step:
                    normed(s + 1)
                body(NG - 1, 1)
                if not first:
                    pe.wait_ge(x_new, s)
                for n in range(2):
                    last = mm(vsum[:, n * 512:(n + 1) * 512], ident[:], x_cur[:, n * 512:(n + 1) * 512], start=True,
                              stop=False, skip_group_check=True)
                last.then_inc(x_taken, 1)

            pe.wait_ge(rows_in, 16 * 8 * DEPTH)
            pe.wait_ge(consts, 3)
            nc.tensor.transpose(bank[:, 0, 0:DEPTH * ROWS], rows[:], ident[0:DEPTH * ROWS, 0:DEPTH * ROWS]).then_inc(rowsT, 1)
            pe.sem_inc(chunk_free, RING)
            pe.sem_inc(u_free, GR)
            pe.sem_inc(v_free, V_START)
            pe.wait_ge(gains_ready, 1)
            normed(0)
            front(0, lambda i, half: None)
            with pe.Fori(1, STEPS - 1) as s:
                front(s, lambda i, half: experts((s - 1) * NG + i, half))
            front(STEPS - 1, lambda i, half: experts((STEPS - 2) * NG + i, half), last_step=True)
            last = (STEPS - 1) * NG
            with pe.Fori(0, NG) as i:
                experts(last + i, 0)
                experts(last + i, 1)


_INS = ["x", "positions", "norm_mix", "w_in", "gm_v_norm", "gm_ws", "gm_b", "gm_out_norm", "mla_q_norm",
        "mla_w_uq", "mla_kv_norm", "mla_w_ukv", "mla_out_norm", "hg_lb_logits", "hg_out_norm", "w_out",
        "norm_ffn", "peer_w_q", "peer_sub_keys", "peer_u", "peer_v", "norm_final"]


def kernel(**inputs):
    import concourse.bacc as bacc
    from concourse.bass_utils import run_bass_kernel_spmd

    nc = bacc.Bacc("TRN2", target_bir_lowering=False, num_devices=1)
    arrays, args = {}, []
    for name in _INS:
        a = np.ascontiguousarray(inputs[name])
        arrays[f"in_{name}"] = a
        args.append(nc.dram_tensor(f"in_{name}", a.shape, mybir.dt.from_np(a.dtype), kind="ExternalInput").ap())
    out = nc.dram_tensor("out_0", (1, SEQ, D), F32, kind="ExternalOutput").ap()
    build(nc, *args, out)
    r = run_bass_kernel_spmd(nc, [arrays], core_ids=[0])
    return r.results[0]["out_0"]
```
